# Optimizing a Trainium2 kernel written in Bass

```python
import math
import jax, jax.numpy as jnp
from jax import lax
import numpy as np

D_MODEL = 1024
BATCH = 1
SEQ = 256
DEPTH = 2

SSM_WIDTH = D_MODEL // 2
SSM_GROUP = 16
SSM_GROUPS = SSM_WIDTH // SSM_GROUP
SSM_STATE = 64
ATTN_WIDTH = D_MODEL - SSM_WIDTH
ATTN_HEAD_DIM = 64
ATTN_HEADS = ATTN_WIDTH // (2 * ATTN_HEAD_DIM)
IN_COLS = SSM_WIDTH + 3 * ATTN_WIDTH
D_FF = 2752
N_EXPERTS = 8
TOP_K = 2
D_FF_EXPERT = 3584
N_DENSE = (DEPTH + 1) // 2
N_MOE = DEPTH // 2
Q_BLOCK = 128
NORM_EPS = 1e-6
STEP_MIN = 1e-3
STEP_MAX = 1e-1

kernel_name = "hymba_style_s5_diffattn_moe_encoder"

def rmsnorm(x, g):
    x32 = x.astype(jnp.float32)
    y = x32 * lax.rsqrt(jnp.mean(x32 * x32, axis=-1, keepdims=True) + NORM_EPS)
    return (y * g.astype(jnp.float32)).astype(x.dtype)

def swiglu(h, w_gate, w_up, w_down):
    return (jax.nn.silu(h @ w_gate) * (h @ w_up)) @ w_down

def alibi_slopes(n_heads):
    return 2.0 ** (-8.0 * jnp.arange(1, n_heads + 1, dtype=jnp.float32) / n_heads)

def _scan_combine(e1, e2):
    a1, b1 = e1
    a2, b2 = e2
    return a1 * a2, a2 * b1 + b2

def ssm_direction(u_c, lam_re, lam_im, log_step, b_re, b_im, c_re, c_im, reverse):
    f32 = jnp.float32
    lam = lax.complex(lam_re.astype(f32), lam_im.astype(f32))
    step = jnp.exp(log_step.astype(f32))[:, None]
    lam_bar = jnp.exp(lam * step)
    b = lax.complex(b_re.astype(f32), b_im.astype(f32))
    b_bar = ((lam_bar - 1.0) / lam)[:, :, None] * b
    c = lax.complex(c_re.astype(f32), c_im.astype(f32))
    bu = jnp.einsum('blgh,gph->blgp', u_c, b_bar)
    a = jnp.broadcast_to(lam_bar, (1, bu.shape[1]) + lam_bar.shape)
    _, states = lax.associative_scan(_scan_combine, (a, bu), reverse=reverse, axis=1)
    return jnp.real(jnp.einsum('blgp,ghp->blgh', states, c))

def ssm_mixer(u, lam_re, lam_im, log_step, b_re, b_im, c_re, c_im, d_skip, w_glu, b_glu, g_out):
    bsz, seq, _ = u.shape
    u32 = u.astype(jnp.float32)
    u_c = u32.reshape(bsz, seq, SSM_GROUPS, SSM_GROUP).astype(jnp.complex64)
    y = u32 * d_skip.astype(jnp.float32)
    for direction, reverse in ((0, False), (1, True)):
        y = y + ssm_direction(u_c, lam_re[direction], lam_im[direction], log_step[direction],
                              b_re[direction], b_im[direction], c_re[direction], c_im[direction],
                              reverse).reshape(bsz, seq, SSM_WIDTH)
    y = jax.nn.gelu(y).astype(u.dtype)
    y = y * jax.nn.sigmoid(y @ w_glu + b_glu)
    return rmsnorm(y, g_out)

def diff_attention(q, k, v, lq1, lk1, lq2, lk2, g_subln, lambda_init):
    f32 = jnp.float32
    bsz, seq, _ = q.shape
    scale = ATTN_HEAD_DIM ** -0.5
    qh = q.astype(f32).reshape(bsz, seq, ATTN_HEADS, 2, ATTN_HEAD_DIM) * scale
    kh = k.astype(f32).reshape(bsz, seq, ATTN_HEADS, 2, ATTN_HEAD_DIM)
    vh = v.astype(f32).reshape(bsz, seq, ATTN_HEADS, 2 * ATTN_HEAD_DIM)
    k1, k2 = kh[..., 0, :], kh[..., 1, :]
    lam = (jnp.exp(jnp.sum(lq1.astype(f32) * lk1.astype(f32)))
           - jnp.exp(jnp.sum(lq2.astype(f32) * lk2.astype(f32))) + lambda_init)
    slopes = alibi_slopes(ATTN_HEADS)
    pos = jnp.arange(seq, dtype=f32)
    n_blocks = seq // Q_BLOCK
    q_blocks = qh.reshape(bsz, n_blocks, Q_BLOCK, ATTN_HEADS, 2, ATTN_HEAD_DIM).transpose(1, 0, 2, 3, 4, 5)
    pos_blocks = pos.reshape(n_blocks, Q_BLOCK)

    def one_block(xs):
        q_blk, p_blk = xs
        bias = -slopes[:, None, None] * jnp.abs(p_blk[:, None] - pos[None, :])
        s1 = jnp.einsum('bqhd,bkhd->bhqk', q_blk[..., 0, :], k1) + bias
        s2 = jnp.einsum('bqhd,bkhd->bhqk', q_blk[..., 1, :], k2) + bias
        attn = jax.nn.softmax(s1, axis=-1) - lam * jax.nn.softmax(s2, axis=-1)
        return jnp.einsum('bhqk,bkhe->bqhe', attn, vh)

    o = lax.map(one_block, (q_blocks, pos_blocks))
    o = o.transpose(1, 0, 2, 3, 4).reshape(bsz, seq, ATTN_HEADS, 2 * ATTN_HEAD_DIM)
    o = rmsnorm(o, g_subln) * (1.0 - lambda_init)
    return o.reshape(bsz, seq, ATTN_WIDTH).astype(q.dtype)

def moe_swiglu(h, w_router, b_router, w_gate, w_up, w_down):
    bsz, seq, dm = h.shape
    t = h.reshape(-1, dm)
    logits = (t @ w_router).astype(jnp.float32) + b_router.astype(jnp.float32)
    top_vals, top_idx = lax.top_k(logits, TOP_K)
    top_w = jax.nn.softmax(top_vals, axis=-1)
    gates = jnp.einsum('nk,nke->ne', top_w,
                       jax.nn.one_hot(top_idx, N_EXPERTS, dtype=jnp.float32)).astype(h.dtype)
    out = jnp.zeros_like(t)
    for e in range(N_EXPERTS):
        out = out + gates[:, e:e + 1] * swiglu(t, w_gate[e], w_up[e], w_down[e])
    return out.reshape(bsz, seq, dm)

def setup_inputs(seed: int = 0) -> dict:
    key = jax.random.key(seed)
    ks = jax.random.split(key, 40)
    f32 = jnp.float32
    nrm = lambda k, shape, s: jax.random.normal(k, shape, f32) * s
    gain = lambda k, shape: 1.0 + 0.02 * jax.random.normal(k, shape, f32)
    n_idx = jnp.arange(SSM_STATE, dtype=f32)
    lam_shape = (DEPTH, 2, SSM_GROUPS, SSM_STATE)
    return {
        "x": jax.random.normal(ks[0], (BATCH, SEQ, D_MODEL), f32),
        "g_mix": gain(ks[1], (DEPTH, D_MODEL)),
        "w_in": nrm(ks[2], (DEPTH, D_MODEL, IN_COLS), D_MODEL ** -0.5),
        "ssm_lambda_re": -0.5 + 0.01 * jax.random.normal(ks[3], lam_shape, f32),
        "ssm_lambda_im": math.pi * n_idx + 0.01 * jax.random.normal(ks[4], lam_shape, f32),
        "ssm_log_step": jax.random.uniform(ks[5], (DEPTH, 2, SSM_GROUPS), f32,
                                           math.log(STEP_MIN), math.log(STEP_MAX)),
        "ssm_b_re": nrm(ks[6], (DEPTH, 2, SSM_GROUPS, SSM_STATE, SSM_GROUP), (2.0 * SSM_GROUP) ** -0.5),
        "ssm_b_im": nrm(ks[7], (DEPTH, 2, SSM_GROUPS, SSM_STATE, SSM_GROUP), (2.0 * SSM_GROUP) ** -0.5),
        "ssm_c_re": nrm(ks[8], (DEPTH, 2, SSM_GROUPS, SSM_GROUP, SSM_STATE), (2.0 * SSM_STATE) ** -0.5),
        "ssm_c_im": nrm(ks[9], (DEPTH, 2, SSM_GROUPS, SSM_GROUP, SSM_STATE), (2.0 * SSM_STATE) ** -0.5),
        "ssm_d": nrm(ks[10], (DEPTH, SSM_WIDTH), 1.0),
        "w_glu": nrm(ks[11], (DEPTH, SSM_WIDTH, SSM_WIDTH), SSM_WIDTH ** -0.5),
        "b_glu": nrm(ks[12], (DEPTH, SSM_WIDTH), 0.02),
        "g_ssm_out": gain(ks[13], (DEPTH, SSM_WIDTH)),
        "lambda_q1": nrm(ks[14], (DEPTH, ATTN_HEAD_DIM), 0.1),
        "lambda_k1": nrm(ks[15], (DEPTH, ATTN_HEAD_DIM), 0.1),
        "lambda_q2": nrm(ks[16], (DEPTH, ATTN_HEAD_DIM), 0.1),
        "lambda_k2": nrm(ks[17], (DEPTH, ATTN_HEAD_DIM), 0.1),
        "g_subln": gain(ks[18], (DEPTH, 2 * ATTN_HEAD_DIM)),
        "w_out": nrm(ks[19], (DEPTH, D_MODEL, D_MODEL), D_MODEL ** -0.5),
        "g_ffn": gain(ks[20], (DEPTH, D_MODEL)),
        "dense_w_gate": nrm(ks[21], (N_DENSE, D_MODEL, D_FF), D_MODEL ** -0.5),
        "dense_w_up": nrm(ks[22], (N_DENSE, D_MODEL, D_FF), D_MODEL ** -0.5),
        "dense_w_down": nrm(ks[23], (N_DENSE, D_FF, D_MODEL), D_FF ** -0.5),
        "w_router": nrm(ks[24], (N_MOE, D_MODEL, N_EXPERTS), D_MODEL ** -0.5),
        "b_router": nrm(ks[25], (N_MOE, N_EXPERTS), 0.01),
        "moe_w_gate": nrm(ks[26], (N_MOE, N_EXPERTS, D_MODEL, D_FF_EXPERT), D_MODEL ** -0.5),
        "moe_w_up": nrm(ks[27], (N_MOE, N_EXPERTS, D_MODEL, D_FF_EXPERT), D_MODEL ** -0.5),
        "moe_w_down": nrm(ks[28], (N_MOE, N_EXPERTS, D_FF_EXPERT, D_MODEL), D_FF_EXPERT ** -0.5),
        "g_final": gain(ks[29], (D_MODEL,)),
    }

def reference(x, g_mix, w_in, ssm_lambda_re, ssm_lambda_im, ssm_log_step, ssm_b_re, ssm_b_im,
              ssm_c_re, ssm_c_im, ssm_d, w_glu, b_glu, g_ssm_out, lambda_q1, lambda_k1,
              lambda_q2, lambda_k2, g_subln, w_out, g_ffn, dense_w_gate, dense_w_up,
              dense_w_down, w_router, b_router, moe_w_gate, moe_w_up, moe_w_down, g_final):
    splits = [SSM_WIDTH, SSM_WIDTH + ATTN_WIDTH, SSM_WIDTH + 2 * ATTN_WIDTH]
    for i in range(DEPTH):
        lambda_init = 0.8 - 0.6 * math.exp(-0.3 * i)
        h = rmsnorm(x, g_mix[i])
        z = h @ w_in[i]
        u, q, k, v = jnp.split(z, splits, axis=-1)
        y_ssm = ssm_mixer(u, ssm_lambda_re[i], ssm_lambda_im[i], ssm_log_step[i],
                          ssm_b_re[i], ssm_b_im[i], ssm_c_re[i], ssm_c_im[i],
                          ssm_d[i], w_glu[i], b_glu[i], g_ssm_out[i])
        y_att = diff_attention(q, k, v, lambda_q1[i], lambda_k1[i], lambda_q2[i], lambda_k2[i],
                               g_subln[i], lambda_init)
        x = x + jnp.concatenate([y_ssm, y_att], axis=-1) @ w_out[i]
        h = rmsnorm(x, g_ffn[i])
        if i % 2 == 0:
            j = i // 2
            x = x + swiglu(h, dense_w_gate[j], dense_w_up[j], dense_w_down[j])
        else:
            j = i // 2
            x = x + moe_swiglu(h, w_router[j], b_router[j], moe_w_gate[j], moe_w_up[j], moe_w_down[j])
    return rmsnorm(x, g_final)


_drawn_inputs = setup_inputs


def setup_inputs(seed=0):
    import zlib

    import numpy as np

    out = dict(_drawn_inputs(seed))
    spreads = {}
    factors = {}
    for name, (base, spread) in spreads.items():
        noise = np.random.default_rng([zlib.crc32(name.encode()), seed]).standard_normal(out[name].shape)
        drawn = base * np.exp(spread * noise) if base else spread * noise
        out[name] = __import__('jax').numpy.asarray(drawn.astype(out[name].dtype))
    for name, factor in factors.items():
        out[name] = (out[name] * factor).astype(out[name].dtype)
    return out
```

```python
import math
from contextlib import ExitStack

import numpy as np

import concourse.bass as bass
from concourse import mybir

ALU = mybir.AluOpType
ACT = mybir.ActivationFunctionType
F32 = mybir.dt.float32
I32 = mybir.dt.int32
AX = mybir.AxisListType

P = 128
D = 1024
KT = D // P
SEQ = 256
TT = SEQ // P
DEPTH = 2
SW = 512
FT = SW // P
GROUP, STATE = 16, 64
NG = SW // GROUP
GP = NG // 2
ST = GP * 2
HEADS, HD = 4, 64
DFF, DFF_E, NE = 2752, 3584, 8
NF_D = -(-DFF // P)
NF_E = DFF_E // P
CAP = P
EPS = 1e-6
ROUND = 1.5 * 2.0 ** 23
INV2PI = 1.0 / (2.0 * math.pi)
TWOPI = 6.283185
GELU_C = math.sqrt(2.0 / math.pi)
LINIT = [0.8 - 0.6 * math.exp(-0.3 * i) for i in range(DEPTH)]
SLOPES = [2.0 ** (-8.0 * (h + 1) / HEADS) for h in range(HEADS)]

C_ID, C_ONE, C_TRI, C_DIST, C_T, C_SLOT, C_E8 = 0, 128, 256, 384, 896, 1152, 1280
C_N = 1296
Q_GMIX, Q_GFFN, Q_D, Q_BGLU, Q_GSSM, Q_GSUB, Q_LRE, Q_LIM, Q_LS, Q_LQ, Q_BR = 0, 8, 16, 20, 24, 28, 29, 61, 93, 125, 381
Q_N = Q_BR + NE
R_GF, R_GM = 0, D

UNITS = ([("norm", "D"), ("norm", "A")] * 2 + [("zu", "A")] * 2 + [("zqkv", "A")] * 6 + [("glu", "A")] * 2
         + [("scores", "D")] * 8 + [("at", "A")] * 4 + [("ot", "A")] * 2 + [("oss", "A")] * 2
         + [("gss", "A")] + [("out", "D")] * 4 + [("fnorm", "D"), ("fnorm", "A")] * 2)
UL = len(UNITS)
FIRST = {}
for _i, (_s, _) in enumerate(UNITS):
    FIRST.setdefault(_s, _i)
RING0, RINGN = 4, 4


def unit(l, stage, k=0):
    return l * UL + FIRST[stage] + k


def emptied(u):
    who = UNITS[u % UL][1]
    return who, (u // UL) * sum(w == who for _, w in UNITS) + sum(w == who for _, w in UNITS[:u % UL + 1])


def bank(u):
    return RING0 + u % RINGN


def encoder(nc, x, consts, rows, params, bmat, cmat, wmix, wglu, wrouter, wdense, wmoe, out):
    with ExitStack() as ctx:
        def sb(name, shape, dt=F32):
            return ctx.enter_context(nc.sbuf_tensor(name, shape, dt))

        def sem(name):
            return ctx.enter_context(nc.semaphore(name))

        ps = ctx.enter_context(nc.psum_tensor("ps", [P, 8, 512], F32))

        X = sb("X", [P, TT, D])
        hn = sb("hn", [P, TT, D])
        hT = sb("hT", [P, KT, SEQ])
        ffw = sb("ffw", [P, 4, 3 * D])
        mixw = sb("mixw", [P, 2, KT, 512])
        cst = sb("cst", [P, C_N])
        par = sb("par", [P, DEPTH, Q_N])
        small = sb("small", [P, 16, ST])
        bw = sb("bw", [P, FT, 2, 2, P])
        row = bw[:].rearrange("p a b c n -> p (a b c n)")
        cw = sb("cw", [P, 2, ST, 32])
        work = sb("work", [P, 28 * SEQ])

        def part(at, *shape):
            names = "abcd"[:len(shape)]
            sizes = dict(zip(names, shape))
            flat = work[:, at * SEQ:at * SEQ + math.prod(shape) * SEQ]
            return flat.rearrange(f"p ({' '.join(names)} t) -> p {' '.join(names)} t", **sizes)

        phase = part(0, 2)
        rnd = part(2, 2)
        frac = part(4, 2)
        trig = part(6, 2, 3)
        ri1 = part(12, 2)
        ri2 = part(14, 2)
        st = part(16, 2, 2)
        ro1 = part(20, 2, 2)
        ro2 = part(24, 2, 2)
        S = part(0, 2, 2, 2)
        A = part(8, 2 * HEADS)
        AT = part(16, HEADS, TT)
        osq = part(24, 2, 2)
        uT = sb("uT", [P, FT, SEQ])
        qT = sb("qT", [P, HEADS, SEQ])
        kT = sb("kT", [P, HEADS, SEQ])
        v = sb("v", [P, TT, 512])
        cat = sb("cat", [P, KT, SEQ])
        yt = sb("yt", [P, FT, SEQ])
        yq = sb("yq", [P, FT, SEQ])
        th = sb("th", [P, FT, SEQ])
        sd = sb("sd", [P, 3, 512])
        col = sb("col", [P, 96])
        hid = sb("hid", [P, 2, SEQ])
        sg = sb("sg", [P, 2, SEQ])
        wr = sb("wr", [P, KT, NE])
        rt = sb("rt", [P, 14, TT, NE])
        cnt = sb("cnt", [1, NE], I32)
        craw = cat[:].rearrange("p (r a) (b n) -> p r (a b) n", r=2, n=32)
        ctmp = yt[:].rearrange("p a (b n) -> p (a b) n", n=32)
        pick = kT[:, 0:2].rearrange("p a (b n) -> p a b n", b=TT)
        wT = v[:, 0, 0:SEQ]
        hg = hT
        ybuf = qT[:].rearrange("p a t -> p (a t)")

        ident = cst[:, C_ID:C_ID + P]
        ones = cst[:, C_ONE:C_ONE + P]

        names = """in_x in_cst in_row in_par in_b in_c in_glu in_wr out_done
            unit_done emptied_act emptied_dve act_chain dve_chain pool_chain
            sumsq rstd hn_ready param_load small_act small_dve small_sin cw_ready
            phase_ready frac_ready trig_ready bu_ready bu_read scanned rot1 rot2 c_done  y_read
            gin gtanh g_ready q_ready qs_ready  score_ready exp_done att_ready sqo rms_o rms_y cat_ready
            gu_done silu_done hid_ready down_done dense_added lg_done routed_exp ex_done picked gathered
            wt_done hg_ready wt_ready acc_act acc_dve scattered added sel_ready pos_done tables_ready
            xh_ready final_ready fin_out lamb_in lamb_ex col_ready""".split()
        s = {n: sem(n) for n in names}
        mix_full = [sem(f"mix_full{i}") for i in range(2)]
        ff_full = [sem(f"ff_full{i}") for i in range(4)]

        block = ctx.enter_context(nc.Block())

        def chunk(l, k):
            return 7 * l + k

        def last_use(c):
            stage, k = [("zu", 1), ("zqkv", 1), ("zqkv", 3), ("zqkv", 5), ("glu", 1), ("out", 1), ("out", 3)][c % 7]
            return unit(c // 7, stage, k)

        def mix_wait(eng, c):
            eng.wait_ge(mix_full[c % 2], 16 * (c // 2 + 1))

        def tile_no(m, f):
            return NF_D + NF_E * m + f

        @block.sync
        def _(sp):
            sp.dma_start(X[:], x).then_inc(s["in_x"], 16)
            sp.dma_start(par[:], params).then_inc(s["in_par"], 16)
            sp.dma_start(cst[:], consts).then_inc(s["in_cst"], 16)

            def mix(l, k):
                c = chunk(l, k)
                if c >= 2:
                    sp.wait_ge(s["unit_done"], last_use(c - 2) + 1)
                if k == 4:
                    sp.dma_start(mixw[:, c % 2, 0:FT], wglu[l]).then_inc(mix_full[c % 2], 16)
                else:
                    sp.dma_start(mixw[:, c % 2], wmix[l, k - (k > 4)]).then_inc(mix_full[c % 2], 16)

            def ffn_tile(src, slot, free=None):
                if free is not None:
                    sp.wait_ge(s["down_done"], free)
                sp.dma_start(ffw[:, slot], src).then_inc(ff_full[slot], 16)

            mix(0, 0)
            mix(0, 1)
            sp.dma_start(wr[:], wrouter).then_inc(s["in_wr"], 16)
            for f in range(4):
                ffn_tile(wdense[f], (f + 2) % 4)
            for k in range(2, 7):
                mix(0, k)
            mix(1, 0)
            mix(1, 1)
            with sp.Fori(1, NF_D // 4) as g:
                for t in range(4):
                    ffn_tile(wdense[bass.ds(4 * g + t, 1)].rearrange("a p n -> p (a n)"), (t + 2) % 4, 4 * g + (t - 3))
            for f in range(NF_D // 4 * 4, NF_D):
                ffn_tile(wdense[f], (f + 2) % 4, f - 3)
            for f in range(4):
                ffn_tile(wmoe[f], f, tile_no(0, f) - 3)
            for k in range(2, 7):
                mix(1, k)
            with sp.Fori(1, NE * NF_E // 4) as g:
                for t in range(4):
                    ffn_tile(wmoe[bass.ds(4 * g + t, 1)].rearrange("a p n -> p (a n)"), t, 4 * g + (tile_no(0, t) - 3))
            sp.wait_ge(s["tables_ready"], 1)
            m = sp.alloc_register("sp_pass")
            sp.reg_mov(m, NE)
            with sp.Fori(0, NE) as e:
                c = sp.value_load(cnt[0:1, bass.ds(e, 1)], min_val=0, max_val=SEQ)
                with sp.If(c > CAP):
                    n = sp.snap(m, min_val=NE, max_val=2 * NE)
                    with sp.Fori(0, NF_E // 4) as g:
                        for t in range(4):
                            ffn_tile(wmoe[bass.ds(NF_E * e + 4 * g + t, 1)].rearrange("a p n -> p (a n)"), t,
                                     NF_E * n + 4 * g + (tile_no(0, t) - 3))
                    sp.reg_add(m, m, 1)
            sp.wait_ge(s["final_ready"], 1)
            sp.dma_start(out, hn[:]).then_inc(s["out_done"], 16)
            sp.wait_ge(s["out_done"], 16)

        @block.gpsimd
        def _(pool):
            for l in range(DEPTH):
                if l:
                    pool.wait_ge(s["bu_ready"], ST)
                pool.dma_start(bw[:], bmat[l]).then_inc(s["in_b"], 16)
                if l:
                    pool.wait_ge(s["hn_ready"], 2)
                pool.dma_start(craw[:], cmat[l]).then_inc(s["in_c"], 16)
                for i in range(ST):
                    n = ST * l + i
                    pool.wait_ge(s["scanned"], n + 1)
                    if n >= 2:
                        pool.wait_ge(s["c_done"], n - 1)
                    nc.gpsimd.tensor_tensor(ro2[:, i % 2], st[:, i % 2, ::-1, :], trig[:, i % 2, 2:0:-1, :],
                                            ALU.mult).then_inc(s["rot2"], 1)
            pool.wait_ge(s["bu_ready"], ST * DEPTH)
            pool.dma_start(row[:], rows).then_inc(s["in_row"], 16)

        @block.scalar
        def _(act):
            chain = [0]

            def link(ins):
                chain[0] += 1
                ins.then_inc(s["act_chain"], 1)
                act.wait_ge(s["act_chain"], chain[0])

            def full(u):
                act.wait_ge(s["unit_done"], u + 1)

            def norm_squares(m):
                for t in range(TT):
                    ins = nc.scalar.activation(hn[:, t], X[:, t], ACT.Square, accum_out=col[:, 2 * t:2 * t + 1])
                ins.then_inc(s["sumsq"], 1)
                act.wait_ge(s["rstd"], 2 * m + 1)
                nc.scalar.activation(col[:, 8:10], col[:, 4:6], ACT.Sqrt).then_inc(s["small_act"], 1)

            def norm_empty(l, stage, gain):
                for k in (1, 3):
                    full(unit(l, stage, k))
                    for j in range(2):
                        f = 2 * k + j
                        ins = nc.scalar.activation(hT[:, f, :], ps[:, bank(unit(l, stage, k)), j * 256:j * 256 + 256],
                                                   ACT.Copy, scale=par[:, l, gain + f:gain + f + 1])
                    ins.then_inc(s["emptied_act"], 1)

            def phases(l, i):
                n = ST * l + i
                act.wait_ge(s["small_dve"], 4 * l + 4)
                if n:
                    act.wait_ge(s["frac_ready"], n)
                nc.scalar.activation(phase[:, 0], cst[:, C_T:C_T + SEQ], ACT.Copy, scale=small[:, 4, i:i + 1])
                link(nc.scalar.activation(phase[:, 1], cst[:, C_T:C_T + SEQ], ACT.Identity, bias=col[:, 17:18],
                                          scale=small[:, 4, i:i + 1]))
                nc.scalar.activation(rnd[:], phase[:], ACT.Copy, bias=ROUND).then_inc(s["phase_ready"], 1)

            def trigs(l, i):
                n = ST * l + i
                act.wait_ge(s["frac_ready"], n + 1)
                if n >= 2:
                    act.wait_ge(s["rot1"], n - 1)
                    act.wait_ge(s["rot2"], n - 1)
                nc.scalar.activation(trig[:, i % 2, 0], frac[:, 1], ACT.Sin, scale=-TWOPI)
                nc.scalar.activation(trig[:, i % 2, 1], frac[:, 0], ACT.Sin, scale=-TWOPI)
                nc.scalar.activation(trig[:, i % 2, 2], frac[:, 0], ACT.Sin, scale=TWOPI).then_inc(s["trig_ready"], 1)

            for l in range(DEPTH):
                if l == 0:
                    act.wait_ge(s["in_par"], 16)
                else:
                    act.wait_ge(s["c_done"], ST * l)
                pr = par[:, l]
                nc.scalar.activation(small[:, 0], pr[:, Q_LS:Q_LS + ST], ACT.Exp).then_inc(s["small_act"], 1)
                act.wait_ge(s["small_dve"], 4 * l + 1)
                nc.scalar.activation(small[:, 3], small[:, 1], ACT.Exp)
                nc.scalar.activation(col[:, 12:14], col[:, 10:12], ACT.Exp).then_inc(s["small_act"], 1)
                act.wait_ge(s["small_dve"], 4 * l + 2)
                nc.scalar.activation(small[:, 5:7], small[:, 7:9], ACT.Sin, scale=-TWOPI).then_inc(s["small_act"], 1)

                if l == 0:
                    act.wait_ge(s["in_x"], 16)
                else:
                    act.wait_ge(s["dense_added"], 1)
                norm_squares(2 * l)
                norm_empty(l, "norm", Q_GMIX)
                for k in range(2):
                    u = unit(l, "zu", k)
                    full(u)
                    nc.scalar.activation(uT[:, 2 * k:2 * k + 2, :], ps[:, bank(u)].rearrange("p (a t) -> p a t", a=2),
                                         ACT.Copy).then_inc(s["emptied_act"], 1)
                phases(l, 0)
                trigs(l, 0)
                for i in range(ST):
                    if i + 1 < ST:
                        phases(l, i + 1)
                        trigs(l, i + 1)
                    if i >= 3 and i % 4 == 3 and i // 4 < 6:
                        k = i // 4
                        u = unit(l, "zqkv", k)
                        full(u)
                        pb = ps[:, bank(u)]
                        if k < 4:
                            dst = (qT, kT)[k // 2][:, 2 * (k % 2):2 * (k % 2) + 2, :]
                            nc.scalar.activation(dst, pb.rearrange("p (a t) -> p a t", a=2), ACT.Copy,
                                                 scale=(HD ** -0.5 if k < 2 else 1.0)).then_inc(s["emptied_act"], 1)
                        else:
                            nc.scalar.activation(v[:, k - 4], pb, ACT.Copy).then_inc(s["emptied_act"], 1)
                    if i % 8 == 7:
                        act.wait_ge(s["gin"], FT * l + i // 8 + 1)
                        nc.scalar.activation(th[:, i // 8], th[:, i // 8], ACT.Tanh,
                                             scale=GELU_C).then_inc(s["gtanh"], 1)
                for k in range(2):
                    u = unit(l, "glu", k)
                    full(u)
                    for j in range(2):
                        f = 2 * k + j
                        ins = nc.scalar.activation(th[:, f], ps[:, bank(u), j * 256:j * 256 + 256], ACT.Tanh,
                                                   bias=col[:, 20 + f:21 + f], scale=0.25)
                    ins.then_inc(s["emptied_act"], 1)
                for k in range(2 * HEADS):
                    act.wait_ge(s["score_ready"], 2 * HEADS * l + k + 1)
                    for q in range(TT):
                        c = 4 * (k // 2 % 2) + 2 * (k % 2) + q
                        ins = nc.scalar.activation(S[:, k // 2 % 2, k % 2, q], S[:, k // 2 % 2, k % 2, q], ACT.Exp,
                                                   bias=col[:, 64 + c:65 + c], accum_out=col[:, 72 + c:73 + c])
                    ins.then_inc(s["exp_done"], 1)
                for h in range(HEADS):
                    u = unit(l, "at", h)
                    full(u)
                    nc.scalar.activation(AT[:, h], ps[:, bank(u)].rearrange("p (k t) -> p k t", k=TT),
                                         ACT.Copy).then_inc(s["emptied_act"], 1)
                for k in range(2):
                    u = unit(l, "ot", k)
                    full(u)
                    pb = ps[:, bank(u)].rearrange("p (a t) -> p a t", a=2)
                    nc.scalar.activation(cat[:, FT + 2 * k:FT + 2 * k + 2, :], pb, ACT.Copy)
                    nc.scalar.activation(osq[:, k], pb, ACT.Square).then_inc(s["emptied_act"], 1)
                for k in range(2):
                    u = unit(l, "oss", k)
                    full(u)
                    nc.scalar.activation(sd[:, k], ps[:, bank(u)], ACT.Sqrt, bias=col[:, 18:19],
                                         scale=1.0 / (2 * HD)).then_inc(s["emptied_act"], 1)
                u = unit(l, "gss")
                full(u)
                nc.scalar.activation(sd[:, 2, 0:SEQ], ps[:, bank(u), 0:SEQ], ACT.Sqrt, bias=col[:, 19:20],
                                     scale=1.0 / SW).then_inc(s["emptied_act"], 1)

                act.wait_ge(s["emptied_dve"], emptied(unit(l, "out", 3))[1])
                norm_squares(2 * l + 1)
                norm_empty(l, "fnorm", Q_GFFN)

                def silu(T, t, w):
                    act.wait_ge(s["gu_done"], T + 1)
                    if not isinstance(T, int) or T >= 2:
                        act.wait_ge(s["hid_ready"], T - 1)
                    nc.scalar.activation(sg[:, t % 2, 0:w], ps[:, t % 2, 0:w], ACT.Silu).then_inc(s["silu_done"], 1)

                if l == 0:
                    for f in range(4):
                        silu(f, f, SEQ)
                    with act.Fori(1, NF_D // 4) as g:
                        for t in range(4):
                            silu(4 * g + t, t, SEQ)
                    for f in range(NF_D // 4 * 4, NF_D):
                        silu(f, f, SEQ)
            act.wait_ge(s["routed_exp"], 1)
            nc.scalar.activation(col[:, 44:46], col[:, 40:42], ACT.Exp).then_inc(s["ex_done"], 1)

            def expert(m):
                act.wait_ge(s["gathered"], m + 1)
                nc.scalar.activation(hg[:, :, 0:CAP], ps[:, 4:6].rearrange("p b (a t) -> p (b a) t", a=4),
                                     ACT.Copy).then_inc(s["hg_ready"], 1)
                act.wait_ge(s["wt_done"], m + 1)
                nc.scalar.activation(wT[:], ps[:, 6, 0:SEQ], ACT.Copy).then_inc(s["wt_ready"], 1)
                with act.Fori(0, NF_E // 4) as g:
                    for t in range(4):
                        silu(NF_E * m + 4 * g + (NF_D + t), t, CAP)
                act.wait_ge(s["down_done"], NF_E * m + (NF_D + NF_E))
                if not isinstance(m, int) or m:
                    act.wait_ge(s["scattered"], 2 * m)
                nc.scalar.activation(ybuf[:, 0:512], ps[:, 2], ACT.Copy).then_inc(s["acc_act"], 1)

            expert(0)
            with act.Fori(1, NE) as e:
                expert(e)
            act.wait_ge(s["tables_ready"], 1)
            m = act.alloc_register("act_pass")
            act.reg_mov(m, NE)
            with act.Fori(0, NE) as e:
                c = act.value_load(cnt[0:1, bass.ds(e, 1)], min_val=0, max_val=SEQ)
                with act.If(c > CAP):
                    expert(act.snap(m, min_val=NE, max_val=2 * NE))
                    act.reg_add(m, m, 1)
            act.wait_ge(s["xh_ready"], 1)
            norm_squares(2 * DEPTH)

        @block.vector
        def _(dve):
            chain = [0]

            def link(ins):
                chain[0] += 1
                ins.then_inc(s["dve_chain"], 1)
                dve.wait_ge(s["dve_chain"], chain[0])

            def full(u):
                dve.wait_ge(s["unit_done"], u + 1)

            ts, tt, stt = nc.vector.tensor_scalar, nc.vector.tensor_tensor, nc.vector.scalar_tensor_tensor

            link(nc.vector.memset(col[:, 17:18], 0.25))
            link(nc.vector.memset(col[:, 18:19], EPS))
            link(nc.vector.memset(col[:, 19:20], 16 * EPS))

            small_acts = [0]

            def small_act():
                small_acts[0] += 1
                dve.wait_ge(s["small_act"], small_acts[0])

            def norm_scale(m):
                dve.wait_ge(s["sumsq"], m + 1)
                ts(col[:, 4:6], col[:, 0:4:2], 1.0 / D, EPS, ALU.mult, ALU.add).then_inc(s["rstd"], 2)
                small_act()
                link(nc.vector.reciprocal(col[:, 6:8], col[:, 8:10]))
                for t in range(TT):
                    ins = ts(hn[:, t], X[:, t], col[:, 6 + t:7 + t], None, ALU.mult)
                ins.then_inc(s["hn_ready"], 1)

            def norm_empty(l, stage, gain):
                for k in (0, 2):
                    u = unit(l, stage, k)
                    full(u)
                    for j in range(2):
                        f = 2 * k + j
                        ins = ts(hT[:, f, :], ps[:, bank(u), j * 256:j * 256 + 256],
                                 par[:, l, gain + f:gain + f + 1], None, ALU.mult)
                    ins.then_inc(s["emptied_dve"], 1)

            def wrap(dst, src, tmp):
                link(ts(tmp, src, ROUND, None, ALU.add))
                link(stt(dst, tmp, ROUND, src, ALU.subtract, ALU.subtract))

            def scalars(l):
                pr = par[:, l]
                sm = small
                small_act()
                link(tt(sm[:, 1], pr[:, Q_LRE:Q_LRE + ST], sm[:, 0], ALU.mult))
                link(tt(A[:, 0, 0:2 * HD].rearrange("p (a d) -> p a d", a=2),
                        pr[:, Q_LQ:Q_LQ + 4 * HD].rearrange("p (a b d) -> p a b d", a=2, b=2)[:, :, 0],
                        pr[:, Q_LQ:Q_LQ + 4 * HD].rearrange("p (a b d) -> p a b d", a=2, b=2)[:, :, 1], ALU.mult))
                nc.vector.reduce_sum(col[:, 10:12], A[:, 0, 0:2 * HD].rearrange("p (a d) -> p a d", a=2),
                                     axis=AX.X).then_inc(s["small_dve"], 1)
                link(tt(sm[:, 2], pr[:, Q_LIM:Q_LIM + ST], sm[:, 0], ALU.mult))
                link(ts(sm[:, 2], sm[:, 2], INV2PI, None, ALU.mult))
                wrap(sm[:, 7], sm[:, 2], sm[:, 9])
                link(ts(sm[:, 4], sm[:, 7], -1.0, None, ALU.mult))
                link(ts(sm[:, 10], sm[:, 4], 0.25, None, ALU.add))
                link(ts(sm[:, 9], sm[:, 10], ROUND, None, ALU.add))
                stt(sm[:, 8], sm[:, 9], ROUND, sm[:, 10], ALU.subtract, ALU.subtract).then_inc(s["small_dve"], 1)
                small_act()
                link(ts(col[:, 14:15], col[:, 13:14], col[:, 12:13], -LINIT[l], ALU.subtract, ALU.add))
                link(ts(col[:, 15:16], pr[:, Q_GSUB:Q_GSUB + 1], 1.0 - LINIT[l], None, ALU.mult))
                link(ts(col[:, 20:24], pr[:, Q_BGLU:Q_BGLU + 4], 0.5, None, ALU.mult))
                small_act()
                lre, lim = pr[:, Q_LRE:Q_LRE + ST], pr[:, Q_LIM:Q_LIM + ST]
                link(tt(sm[:, 9], sm[:, 3], sm[:, 6], ALU.mult))
                link(ts(sm[:, 9], sm[:, 9], -1.0, None, ALU.add))
                link(tt(sm[:, 10], sm[:, 3], sm[:, 5], ALU.mult))
                link(tt(sm[:, 11], lre, lre, ALU.mult))
                link(tt(sm[:, 12], lim, lim, ALU.mult))
                link(tt(sm[:, 11], sm[:, 11], sm[:, 12], ALU.add))
                link(nc.vector.reciprocal(sm[:, 11], sm[:, 11]))
                link(tt(sm[:, 12], sm[:, 9], lre, ALU.mult))
                link(tt(sm[:, 13], sm[:, 10], lim, ALU.mult))
                link(tt(sm[:, 12], sm[:, 12], sm[:, 13], ALU.add))
                link(tt(sm[:, 14], sm[:, 12], sm[:, 11], ALU.mult))
                link(tt(sm[:, 12], sm[:, 10], lre, ALU.mult))
                link(tt(sm[:, 13], sm[:, 9], lim, ALU.mult))
                link(tt(sm[:, 12], sm[:, 12], sm[:, 13], ALU.subtract))
                link(tt(sm[:, 15], sm[:, 12], sm[:, 11], ALU.mult))
                ts(sm[:, 0], sm[:, 15], -1.0, None, ALU.mult).then_inc(s["small_dve"], 2)

            def fold_c(l):
                sm = small

                def b(r):
                    return sm[:, r, :].rearrange("p (t a) -> p t a", a=1).to_broadcast([P, ST, 32])
                dve.wait_ge(s["small_dve"], 4 * l + 4)
                dve.wait_ge(s["in_c"], 16 * (l + 1))
                link(tt(cw[:, 0], craw[:, 0], b(14), ALU.mult))
                link(tt(ctmp[:], craw[:, 1], b(15), ALU.mult))
                link(tt(cw[:, 0], cw[:, 0], ctmp[:], ALU.subtract))
                link(tt(cw[:, 1], craw[:, 0], b(0), ALU.mult))
                link(tt(ctmp[:], craw[:, 1], b(14), ALU.mult))
                tt(cw[:, 1], cw[:, 1], ctmp[:], ALU.subtract).then_inc(s["cw_ready"], 1)

            def fracs(l, i):
                n = ST * l + i
                dve.wait_ge(s["phase_ready"], n + 1)
                if n:
                    dve.wait_ge(s["trig_ready"], n)
                stt(frac[:], rnd[:], ROUND, phase[:], ALU.subtract, ALU.subtract).then_inc(s["frac_ready"], 1)

            def gelu(l, ft):
                dve.wait_ge(s["c_done"], ST * l + 8 * (ft + 1))
                y = yt[:, ft]
                ins = stt(y, uT[:, ft], par[:, l, Q_D + ft:Q_D + ft + 1], ps[:, 2 + ft % 2, 0:SEQ],
                          ALU.mult, ALU.add)
                ins.then_inc(s["y_read"], 1)
                dve.wait_ge(s["y_read"], FT * l + ft + 1)
                link(tt(th[:, ft], y, y, ALU.mult))
                link(ts(th[:, ft], th[:, ft], 0.044715, 1.0, ALU.mult, ALU.add))
                tt(th[:, ft], th[:, ft], y, ALU.mult).then_inc(s["gin"], 1)
                dve.wait_ge(s["gtanh"], FT * l + ft + 1)
                stt(yq[:, ft], th[:, ft], 1.0, y, ALU.add, ALU.mult).then_inc(s["g_ready"], 1)

            def state_tile(l, i):
                n = ST * l + i
                b = i % 2
                dve.wait_ge(s["trig_ready"], n + 1)
                dve.wait_ge(s["bu_ready"], n + 1)
                bu = ps[:, b].rearrange("p (r t) -> p r t", r=2)
                cos2 = trig[:, b, 0:1, :].to_broadcast([P, 2, SEQ])
                tt(ri1[:], bu, cos2, ALU.mult)
                link(tt(ri2[:], bu[:, ::-1, :], trig[:, b, 1:3, :], ALU.mult))
                ins = tt(ri1[:], ri1[:], ri2[:], ALU.add)
                ins.then_inc(s["bu_read"], 1)
                dve.wait_ge(s["bu_read"], n + 1)
                if n >= 2:
                    dve.wait_ge(s["rot2"], n - 1)
                decay = small[:, 3, i:i + 1].to_broadcast([P, SEQ])
                for r in range(2):
                    ins = nc.vector.tensor_tensor_scan(st[:, b, r], decay, ri1[:, r], 0.0, ALU.mult, ALU.add)
                ins.then_inc(s["scanned"], 1)
                dve.wait_ge(s["scanned"], n + 1)
                if n >= 2:
                    dve.wait_ge(s["c_done"], n - 1)
                tt(ro1[:, b], st[:, b], cos2, ALU.mult).then_inc(s["rot1"], 1)

            def score(l, k):
                u = unit(l, "scores", k)
                full(u)
                h, m = k // 2, k % 2
                Sk = S[:, h % 2, m]
                if h >= 2:
                    dve.wait_ge(s["att_ready"], HEADS * l + h - 1)
                dist = cst[:, C_DIST:C_DIST + TT * SEQ].rearrange("p (a t) -> p a t", a=TT)
                stt(Sk, dist, -SLOPES[h], ps[:, bank(u)].rearrange("p (a t) -> p a t", a=TT),
                    ALU.mult, ALU.add).then_inc(s["emptied_dve"], 1)
                dve.wait_ge(s["emptied_dve"], emptied(u)[1])
                c = 64 + 4 * (h % 2) + 2 * m
                link(nc.vector.reduce_max(col[:, 34:36], Sk, axis=AX.X))
                ts(col[:, c:c + 2], col[:, 34:36], -1.0, None, ALU.mult).then_inc(s["score_ready"], 1)

            def attend(l, h):
                b = h % 2
                dve.wait_ge(s["exp_done"], 2 * (HEADS * l + h + 1))
                if h:
                    dve.wait_ge(s["att_ready"], HEADS * l + h)
                link(nc.vector.reciprocal(col[:, 80:84], col[:, 72 + 4 * b:76 + 4 * b]))
                link(ts(col[:, 82:84], col[:, 82:84], col[:, 14:15], None, ALU.mult))
                for q in range(TT):
                    ins = ts(A[:, 2 * h + q], S[:, b, 1, q], col[:, 82 + q:83 + q], None, ALU.mult)
                link(ins)
                for q in range(TT):
                    ins = stt(A[:, 2 * h + q], S[:, b, 0, q], col[:, 80 + q:81 + q], A[:, 2 * h + q],
                              ALU.mult, ALU.add)
                ins.then_inc(s["att_ready"], 1)

            for l in range(DEPTH):
                if l == 0:
                    dve.wait_ge(s["in_par"], 16)
                    dve.wait_ge(s["in_x"], 16)
                scalars(l)
                norm_scale(2 * l)
                fold_c(l)
                norm_empty(l, "norm", Q_GMIX)
                fracs(l, 0)
                for i in range(ST):
                    if i + 1 < ST:
                        fracs(l, i + 1)
                    state_tile(l, i)
                    if i % 8 == 7 and i + 1 < ST:
                        gelu(l, i // 8)
                gelu(l, FT - 1)
                for k in range(2):
                    who, n = emptied(unit(l, "glu", k))
                    dve.wait_ge(s["emptied_act"], n)
                    f = slice(2 * k, 2 * k + 2)
                    link(stt(yt[:, f], th[:, f], 1.0, yq[:, f], ALU.add, ALU.mult))
                    ins = tt(th[:, f], yt[:, f], yt[:, f], ALU.mult)
                ins.then_inc(s["qs_ready"], 1)
                score(l, 0)
                score(l, 1)
                for h in range(HEADS):
                    if h + 1 < HEADS:
                        score(l, 2 * h + 2)
                        score(l, 2 * h + 3)
                    attend(l, h)
                for k in range(2):
                    dve.wait_ge(s["emptied_act"], emptied(unit(l, "oss", k))[1])
                    link(nc.vector.reciprocal(sd[:, k], sd[:, k]))
                    f = slice(FT + 2 * k, FT + 2 * k + 2)
                    stt(cat[:, f], cat[:, f], col[:, 15:16], sd[:, k].rearrange("p (a t) -> p a t", a=2),
                        ALU.mult, ALU.mult)
                dve.wait_ge(s["emptied_act"], emptied(unit(l, "gss"))[1])
                link(nc.vector.reciprocal(sd[:, 2, 0:SEQ], sd[:, 2, 0:SEQ]))
                for f in range(FT):
                    ins = stt(cat[:, f], yt[:, f], par[:, l, Q_GSSM + f:Q_GSSM + f + 1], sd[:, 2, 0:SEQ],
                              ALU.mult, ALU.mult)
                ins.then_inc(s["cat_ready"], 1)
                for k in range(4):
                    u = unit(l, "out", k)
                    full(u)
                    xs = X[:, k % 2, (k // 2) * 512:(k // 2) * 512 + 512]
                    tt(xs, xs, ps[:, bank(u)], ALU.add).then_inc(s["emptied_dve"], 1)
                norm_scale(2 * l + 1)
                norm_empty(l, "fnorm", Q_GFFN)

                def hidden(T, t, w, up):
                    dve.wait_ge(s["silu_done"], T + 1)
                    if not isinstance(T, int) or T >= 2:
                        dve.wait_ge(s["down_done"], T - 1)
                    tt(hid[:, t % 2, 0:w], sg[:, t % 2, 0:w], ps[:, t % 2, up:up + w],
                       ALU.mult).then_inc(s["hid_ready"], 1)

                if l == 0:
                    for f in range(4):
                        hidden(f, f, SEQ, SEQ)
                    with dve.Fori(1, NF_D // 4) as g:
                        for t in range(4):
                            hidden(4 * g + t, t, SEQ, SEQ)
                    for f in range(NF_D // 4 * 4, NF_D):
                        hidden(f, f, SEQ, SEQ)
                    dve.wait_ge(s["down_done"], NF_D)
                    for t in range(TT):
                        xs = X[:, t].rearrange("p (a n) -> p a n", a=2)
                        ins = tt(xs, xs, ps[:, 2 + 2 * t:4 + 2 * t], ALU.add)
                    ins.then_inc(s["dense_added"], 1)
                    dve.wait_ge(s["dense_added"], 1)

            dve.wait_ge(s["in_row"], 16)
            full(unit(DEPTH - 1, "fnorm", 3))
            for t in range(TT):
                link(tt(hn[:, t], hn[:, t], row[:, R_GM:R_GM + D], ALU.mult))
            dve.wait_ge(s["lg_done"], 1)
            e8 = cst[:, C_E8:C_E8 + 16].rearrange("p (a e) -> p a e", a=TT)
            lg, oh0, oh1, tmp, sel, gate = (rt[:, j] for j in range(6))

            def wide(c):
                return col[:, c:c + TT].rearrange("p (a b) -> p a b", b=1).to_broadcast([P, TT, NE])

            def largest(val, onehot):
                link(nc.vector.reduce_max(col[:, val:val + TT], lg, axis=AX.X))
                link(tt(tmp, lg, wide(val), ALU.is_equal))
                link(tt(tmp, tmp, e8, ALU.mult))
                link(nc.vector.tensor_reduce(col[:, 48:50], tmp, axis=AX.X, op=ALU.min))
                link(tt(onehot, e8, wide(48), ALU.is_equal))

            lgp = ps[:, 4, 0:TT * NE].rearrange("p (a e) -> p a e", a=TT)
            br = par[:, 0, Q_BR:Q_BR + NE].rearrange("p (a e) -> p a e", a=1).to_broadcast([P, TT, NE])
            link(tt(lg, lgp, br, ALU.add))
            largest(50, oh0)
            link(stt(lg, oh0, -3.0e38, lg, ALU.mult, ALU.add))
            largest(52, oh1)
            tt(col[:, 40:42], col[:, 52:54], col[:, 50:52], ALU.subtract).then_inc(s["routed_exp"], 1)
            tt(sel, oh0, oh1, ALU.add).then_inc(s["sel_ready"], 1)
            dve.wait_ge(s["ex_done"], 1)
            link(ts(col[:, 42:44], col[:, 44:46], 1.0, None, ALU.add))
            link(nc.vector.reciprocal(col[:, 54:56], col[:, 42:44]))
            link(tt(col[:, 56:58], col[:, 44:46], col[:, 54:56], ALU.mult))
            link(tt(gate, oh0, wide(54), ALU.mult))
            link(tt(tmp, oh1, wide(56), ALU.mult))
            link(tt(gate, gate, tmp, ALU.add))
            dve.wait_ge(s["pos_done"], 1)
            pos = ps[:, 5, 0:TT * NE].rearrange("p (a e) -> p a e", a=TT)
            link(ts(rt[:, 6], pos, 1.0, None, ALU.add))
            link(tt(rt[:, 6], rt[:, 6], sel, ALU.mult))
            link(ts(rt[:, 7], rt[:, 6], -1.0 - CAP, None, ALU.add))
            link(ts(rt[:, 6], rt[:, 6], -1.0, None, ALU.add))
            nc.vector.tensor_copy(cnt[:], ps[0:1, 5, TT * NE:TT * NE + NE]).then_inc(s["tables_ready"], 1)
            dve.wait_ge(s["tables_ready"], 1)

            def expert(m, e, part):
                if not isinstance(m, int) or m:
                    dve.wait_ge(s["wt_done"], m)
                slot = cst[:, C_SLOT:C_SLOT + CAP]
                e = slice(e, e + 1) if isinstance(e, int) else bass.ds(e, 1)
                for t in range(TT):
                    ts(pick[:, 0, t], slot, rt[:, 6 + part, t, e], None, ALU.is_equal)
                    ins = ts(pick[:, 1, t], slot, rt[:, 6 + part, t, e], rt[:, 5, t, e], ALU.is_equal, ALU.mult)
                ins.then_inc(s["picked"], 1)
                with dve.Fori(0, NF_E // 4) as g:
                    for t in range(4):
                        hidden(NF_E * m + 4 * g + (NF_D + t), t, CAP, CAP)
                dve.wait_ge(s["down_done"], NF_E * m + (NF_D + NF_E))
                nc.vector.tensor_copy(ybuf[:, 512:D], ps[:, 3]).then_inc(s["acc_dve"], 1)
                for t in range(TT):
                    dve.wait_ge(s["scattered"], 2 * m + (t + 1))
                    xs = X[:, t].rearrange("p (a n) -> p a n", a=2)
                    tt(xs, xs, ps[:, 4 + 2 * t:6 + 2 * t], ALU.add).then_inc(s["added"], 1)

            expert(0, 0, 0)
            with dve.Fori(1, NE) as e:
                expert(e, e, 0)
            m = dve.alloc_register("dve_pass")
            dve.reg_mov(m, NE)
            with dve.Fori(0, NE) as e:
                c = dve.value_load(cnt[0:1, bass.ds(e, 1)], min_val=0, max_val=SEQ)
                with dve.If(c > CAP):
                    expert(dve.snap(m, min_val=NE, max_val=2 * NE), e, 1)
                    dve.reg_add(m, m, 1)

            nc.vector.memset(col[:, 60:61], 0.0).then_inc(s["xh_ready"], 1)
            norm_scale(2 * DEPTH)
            dve.wait_ge(s["hn_ready"], 2 * DEPTH + 1)
            for t in range(TT):
                ins = tt(hn[:, t], hn[:, t], row[:, R_GF:R_GF + D], ALU.mult)
            ins.then_inc(s["final_ready"], 1)

        @block.tensor
        def _(pe):
            mm = nc.tensor.matmul

            def free(u):
                if u >= RINGN:
                    who, n = emptied(u - RINGN)
                    pe.wait_ge(s["emptied_act" if who == "A" else "emptied_dve"], n)

            def empty_wait(u):
                who, n = emptied(u)
                pe.wait_ge(s["emptied_act" if who == "A" else "emptied_dve"], n)

            def norm(l, stage, m):
                pe.wait_ge(s["hn_ready"], m + 1)
                for k in range(4):
                    u = unit(l, stage, k)
                    free(u)
                    for j in range(2):
                        for t in range(TT):
                            f = 2 * k + j
                            ins = nc.tensor.transpose(ps[:, bank(u), j * 256 + t * P:j * 256 + (t + 1) * P],
                                                      hn[:, t, f * P:(f + 1) * P], ident)
                    ins.then_inc(s["unit_done"], 1)

            def ht_ready(l, stage):
                empty_wait(unit(l, stage, 2))
                empty_wait(unit(l, stage, 3))

            def project(l, u, c, k):
                free(u)
                for j in range(2):
                    n = 2 * k + j
                    for f in range(KT):
                        ins = mm(ps[:, bank(u), j * 256:j * 256 + 256], mixw[:, c % 2, f, n * P:(n + 1) * P],
                                 hT[:, f, :], start=(f == 0), stop=(f == KT - 1))
                ins.then_inc(s["unit_done"], 1)
                return ins

            def bu(l, i):
                n = ST * l + i
                if n >= 2:
                    pe.wait_ge(s["bu_read"], n - 1)
                gp, d = i // 2, i % 2
                ft, q = gp // 4, 32 * (gp % 4)
                u = uT[q:q + 32, ft, ::-1] if d else uT[q:q + 32, ft, :]
                for r in range(2):
                    ins = mm(ps[:, i % 2, r * 256:r * 256 + 256], bw[q:q + 32, ft, d, r, :], u, start=True, stop=True,
                             tile_position=(q, 0))
                ins.then_inc(s["bu_ready"], 1)

            def outputs(l, i):
                n = ST * l + i
                gp, d = i // 2, i % 2
                ft, q = gp // 4, 32 * (gp % 4)
                if i % 8 == 0 and FT * l + ft >= 2:
                    pe.wait_ge(s["y_read"], FT * l + ft - 1)
                pe.wait_ge(s["rot1"], n + 1)
                pe.wait_ge(s["rot2"], n + 1)
                for k, src in enumerate((ro1, ro2)):
                    for r in range(2):
                        a = src[:, i % 2, r, ::-1] if d else src[:, i % 2, r, :]
                        ins = mm(ps[q:q + 32, 2 + ft % 2, 0:SEQ], cw[:, r, i, :], a,
                                 start=(d == 0 and k == 0 and r == 0), stop=(d == 1 and k == 1 and r == 1),
                                 tile_position=(0, q))
                ins.then_inc(s["c_done"], 1)

            def zqkv(l, k):
                u = unit(l, "zqkv", k)
                if k % 2 == 0:
                    mix_wait(pe, chunk(l, 1 + k // 2))
                if k < 4:
                    project(l, u, chunk(l, 1 + k // 2), k % 2)
                else:
                    free(u)
                    t = k - 4
                    for f in range(KT):
                        ins = mm(ps[:, bank(u), :], hT[:, f, t * P:(t + 1) * P], mixw[:, chunk(l, 3) % 2, f, :],
                                 start=(f == 0), stop=(f == KT - 1))
                    ins.then_inc(s["unit_done"], 1)

            def gate_up(T, t, w, src):
                slot = (t + 2) % 4 if w == SEQ else t
                pe.wait_ge(ff_full[slot], full_count(T, t, w))
                if not isinstance(T, int) or T >= 2:
                    pe.wait_ge(s["hid_ready"], T - 1)
                for g in range(2):
                    for f in range(KT):
                        ins = mm(ps[:, t % 2, g * w:(g + 1) * w], ffw[:, slot, (g * KT + f) * P:(g * KT + f + 1) * P],
                                 src[:, f, 0:w], start=(f == 0), stop=(f == KT - 1))
                ins.then_inc(s["gu_done"], 1)

            def full_count(T, t, w):
                if w == SEQ:
                    return 16 * (T // 4 + 1) if isinstance(T, int) else (T - t) * 4 + 16
                held = (NF_D + 2 - t - 1) // 4 + 1 if t < 2 else NF_D // 4
                held = sum((f + 2) % 4 == t for f in range(NF_D))
                return (T - (NF_D + t)) * 4 + 16 * (held + 1)

            def down(T, t, w, first, last):
                slot = (t + 2) % 4 if w == SEQ else t
                pe.wait_ge(s["hid_ready"], T + 1)
                for k in range(w // P):
                    for n in range(2):
                        ins = mm(ps[:, 2 + 2 * k + n], hid[:, t % 2, k * P:(k + 1) * P],
                                 ffw[:, slot, 2 * D + n * 512:2 * D + (n + 1) * 512], start=first, stop=last)
                ins.then_inc(s["down_done"], 1)

            def stream(base, nf, w, src):
                gate_up(base + 0, 0, w, src)
                groups = (nf - 1) // 4

                def four(T0, first):
                    for t in range(4):
                        gate_up(T0 + (t + 1), (t + 1) % 4, w, src)
                        down(T0 + t, t, w, first and t == 0, False)
                four(base + 0, True)
                with pe.Fori(1, groups) as g:
                    four(4 * g + base, False)
                n = nf - 4 * groups
                for t in range(n):
                    if t + 1 < n:
                        gate_up(base + (4 * groups + t + 1), t + 1, w, src)
                    down(base + (4 * groups + t), t, w, False, t == n - 1)

            for l in range(DEPTH):
                if l == 0:
                    pe.wait_ge(s["in_cst"], 16)
                norm(l, "norm", 2 * l)
                ht_ready(l, "norm")
                mix_wait(pe, chunk(l, 0))
                for k in range(2):
                    project(l, unit(l, "zu", k), chunk(l, 0), k)
                empty_wait(unit(l, "zu", 1))
                pe.wait_ge(s["in_b"], 16 * (l + 1))
                bu(l, 0)
                pe.wait_ge(s["cw_ready"], l + 1)
                for i in range(ST):
                    if i + 1 < ST:
                        bu(l, i + 1)
                    if i >= 2 and i % 4 == 2 and i // 4 < 6:
                        zqkv(l, i // 4)
                    outputs(l, i)
                c = chunk(l, 4)
                mix_wait(pe, c)
                pe.wait_ge(s["g_ready"], FT * (l + 1))
                for k in range(2):
                    u = unit(l, "glu", k)
                    free(u)
                    for j in range(2):
                        n = 2 * k + j
                        for f in range(FT):
                            ins = mm(ps[:, bank(u), j * 256:j * 256 + 256], mixw[:, c % 2, f, n * P:(n + 1) * P],
                                     yq[:, f], start=(f == 0), stop=(f == FT - 1))
                    ins.then_inc(s["unit_done"], 1)
                for k in range(2 * HEADS):
                    u = unit(l, "scores", k)
                    free(u)
                    h, m = k // 2, k % 2
                    r = slice(HD * m, HD * m + HD)
                    for q in range(TT):
                        ins = mm(ps[:, bank(u), q * 256:q * 256 + 256], qT[r, h, q * P:(q + 1) * P], kT[r, h, :],
                                 start=True, stop=True)
                    ins.then_inc(s["unit_done"], 1)
                for h in range(HEADS):
                    u = unit(l, "at", h)
                    free(u)
                    pe.wait_ge(s["att_ready"], HEADS * l + h + 1)
                    for kt in range(TT):
                        for q in range(TT):
                            ins = nc.tensor.transpose(ps[:, bank(u), kt * 256 + q * P:kt * 256 + (q + 1) * P],
                                                      A[:, 2 * h + q, kt * P:(kt + 1) * P], ident)
                    ins.then_inc(s["unit_done"], 1)
                for k in range(2):
                    u = unit(l, "ot", k)
                    free(u)
                    for j in range(2):
                        h = 2 * k + j
                        empty_wait(unit(l, "at", h))
                        for kt in range(TT):
                            ins = mm(ps[:, bank(u), j * 256:j * 256 + 256], v[:, kt, h * P:(h + 1) * P], AT[:, h, kt],
                                     start=(kt == 0), stop=(kt == TT - 1))
                    ins.then_inc(s["unit_done"], 1)
                for k in range(2):
                    u = unit(l, "oss", k)
                    free(u)
                    empty_wait(unit(l, "ot", k))
                    mm(ps[:, bank(u), :], ones, osq[:, k].rearrange("p a t -> p (a t)"), start=True,
                       stop=True).then_inc(s["unit_done"], 1)
                u = unit(l, "gss")
                free(u)
                pe.wait_ge(s["qs_ready"], l + 1)
                for f in range(FT):
                    ins = mm(ps[:, bank(u), 0:SEQ], ones, th[:, f], start=(f == 0), stop=(f == FT - 1))
                ins.then_inc(s["unit_done"], 1)
                pe.wait_ge(s["cat_ready"], l + 1)
                for k in range(4):
                    u = unit(l, "out", k)
                    c = chunk(l, 5 + k // 2)
                    if k % 2 == 0:
                        mix_wait(pe, c)
                    free(u)
                    t = k % 2
                    for f in range(KT):
                        ins = mm(ps[:, bank(u), :], cat[:, f, t * P:(t + 1) * P], mixw[:, c % 2, f, :],
                                 start=(f == 0), stop=(f == KT - 1))
                    ins.then_inc(s["unit_done"], 1)
                norm(l, "fnorm", 2 * l + 1)
                ht_ready(l, "fnorm")
                if l == 0:
                    stream(0, NF_D, SEQ, hT)

            pe.wait_ge(s["in_wr"], 16)
            for t in range(TT):
                for f in range(KT):
                    ins = mm(ps[:, 4, t * NE:(t + 1) * NE], hT[:, f, t * P:(t + 1) * P], wr[:, f, :],
                             start=(f == 0), stop=(f == KT - 1))
            ins.then_inc(s["lg_done"], 1)
            pe.wait_ge(s["sel_ready"], 1)
            tri = cst[:, C_TRI:C_TRI + P]
            mm(ps[:, 5, 0:NE], tri, rt[:, 4, 0], start=True, stop=True)
            mm(ps[:, 5, NE:2 * NE], ones, rt[:, 4, 0], start=True, stop=False)
            mm(ps[:, 5, NE:2 * NE], tri, rt[:, 4, 1], start=False, stop=True)
            mm(ps[:, 5, 2 * NE:3 * NE], ones, rt[:, 4, 0], start=True, stop=False)
            mm(ps[:, 5, 2 * NE:3 * NE], ones, rt[:, 4, 1], start=False, stop=True).then_inc(s["pos_done"], 1)

            def expert(m):
                pe.wait_ge(s["picked"], m + 1)
                if not isinstance(m, int) or m:
                    pe.wait_ge(s["added"], 2 * m)
                for f in range(KT):
                    for t in range(TT):
                        ins = mm(ps[:, 4 + f // 4, (f % 4) * P:(f % 4 + 1) * P], hn[:, t, f * P:(f + 1) * P],
                                 pick[:, 0, t], start=(t == 0), stop=(t == TT - 1))
                ins.then_inc(s["gathered"], 1)
                for t in range(TT):
                    ins = nc.tensor.transpose(ps[:, 6, t * P:(t + 1) * P], pick[:, 1, t], ident)
                ins.then_inc(s["wt_done"], 1)
                pe.wait_ge(s["hg_ready"], m + 1)
                if not isinstance(m, int) or m:
                    pe.wait_ge(s["acc_act"], m)
                    pe.wait_ge(s["acc_dve"], m)
                stream(NF_E * m + NF_D, NF_E, CAP, hg)
                pe.wait_ge(s["wt_ready"], m + 1)
                pe.wait_ge(s["acc_act"], m + 1)
                pe.wait_ge(s["acc_dve"], m + 1)
                for t in range(TT):
                    for n in range(2):
                        ins = mm(ps[:, 4 + 2 * t + n], wT[:, t * P:(t + 1) * P], ybuf[:, n * 512:(n + 1) * 512],
                                 start=True, stop=True)
                    ins.then_inc(s["scattered"], 1)

            expert(0)
            with pe.Fori(1, NE) as e:
                expert(e)
            pe.wait_ge(s["tables_ready"], 1)
            m = pe.alloc_register("pe_pass")
            pe.reg_mov(m, NE)
            with pe.Fori(0, NE) as e:
                c = pe.value_load(cnt[0:1, bass.ds(e, 1)], min_val=0, max_val=SEQ)
                with pe.If(c > CAP):
                    expert(pe.snap(m, min_val=NE, max_val=2 * NE))
                    pe.reg_add(m, m, 1)


def constants():
    c = np.zeros((P, C_N), np.float32)
    p = np.arange(P)
    c[:, C_ID:C_ID + P] = np.eye(P)
    c[:, C_ONE:C_ONE + P] = 1.0
    c[:, C_TRI:C_TRI + P] = p[:, None] < p[None, :]
    for q in range(TT):
        c[:, C_DIST + q * SEQ:C_DIST + (q + 1) * SEQ] = np.abs(p[:, None] + q * P - np.arange(SEQ)[None, :])
    c[:, C_T:C_T + SEQ] = np.arange(SEQ)
    c[:, C_SLOT:C_SLOT + P] = p
    c[:, C_E8:C_E8 + 16] = np.tile(np.arange(NE) - NE, 2)
    return c


def kernel(**inputs):
    import concourse.bacc as bacc
    from concourse.bass_utils import run_bass_kernel_spmd

    a = {k: np.asarray(v) for k, v in inputs.items()}
    f32 = np.float32

    def by_feature(g, n):
        return g.reshape(DEPTH, n, P).transpose(0, 2, 1)

    def by_state(g):
        return g.reshape(DEPTH, 2, GP, 2, STATE).transpose(0, 3, 4, 2, 1).reshape(DEPTH, P, ST)

    def on_all(r):
        return np.broadcast_to(r[:, None, :], (r.shape[0], P, r.shape[1]))

    step = np.broadcast_to(a["ssm_log_step"][..., None], a["ssm_lambda_re"].shape)
    par = np.concatenate([
        by_feature(a["g_mix"], KT), by_feature(a["g_ffn"], KT), by_feature(a["ssm_d"], FT),
        by_feature(a["b_glu"], FT), by_feature(a["g_ssm_out"], FT), by_feature(a["g_subln"], 1),
        by_state(a["ssm_lambda_re"]), by_state(a["ssm_lambda_im"]), by_state(step),
        on_all(np.concatenate([a["lambda_q1"], a["lambda_k1"], a["lambda_q2"], a["lambda_k2"]], 1)),
        on_all(np.broadcast_to(a["b_router"], (DEPTH, NE)))], 2)
    rows = on_all(np.concatenate([a["g_final"], a["g_ffn"][1]])[None])[0]

    bmat = np.zeros((DEPTH, 4, 2, GROUP, FT, 2, 2, 2, STATE), f32)
    cmat = np.zeros((DEPTH, 2, STATE, 2, FT, 4, 2, 2, GROUP), f32)
    for r, (b, c) in enumerate((("ssm_b_re", "ssm_c_re"), ("ssm_b_im", "ssm_c_im"))):
        b6 = a[b].reshape(DEPTH, 2, FT, 4, 2, STATE, GROUP)
        c6 = a[c].reshape(DEPTH, 2, FT, 4, 2, GROUP, STATE)
        for g in range(2):
            bmat[:, :, g, :, :, :, r, g, :] = b6[:, :, :, :, g].transpose(0, 3, 5, 2, 1, 4)
            cmat[:, g, :, r, :, :, :, g, :] = c6[:, :, :, :, g].transpose(0, 5, 2, 3, 1, 4)
    bmat = bmat.reshape(DEPTH, P, FT, 2, 2, P)
    cmat = cmat.reshape(DEPTH, P, 2, ST, 32)

    def chunks(w, kt, n):
        return w.reshape(DEPTH, kt, P, n, 512).transpose(0, 3, 2, 1, 4)

    wmix = np.concatenate([chunks(a["w_in"], KT, 4), chunks(a["w_out"], KT, 2)], 1)
    wglu = chunks(a["w_glu"], FT, 1)[:, 0]
    wrouter = a["w_router"][0].reshape(KT, P, NE).transpose(1, 0, 2)

    def ffn(gate, up, down, nf):
        n, _, dff = gate.shape
        w = np.zeros((n, nf, P, 3, KT, P), f32)
        pad = nf * P - dff
        for j, g in enumerate((gate, up)):
            g = np.pad(g, ((0, 0), (0, 0), (0, pad))) if pad else g
            w[:, :, :, j] = g.reshape(n, KT, P, nf, P).transpose(0, 3, 2, 1, 4)
        dn = np.pad(down, ((0, 0), (0, pad), (0, 0))) if pad else down
        w[:, :, :, 2] = dn.reshape(n, nf, P, KT, P)
        return w.reshape(n * nf, P, 3 * D)

    wdense = ffn(a["dense_w_gate"], a["dense_w_up"], a["dense_w_down"], NF_D)
    wmoe = ffn(a["moe_w_gate"][0], a["moe_w_up"][0], a["moe_w_down"][0], NF_E)
    arrays = {
        "x_in": a["x"][0].reshape(TT, P, D).transpose(1, 0, 2),
        "consts": constants(), "rows": rows, "params": par.transpose(1, 0, 2), "bmat": bmat, "cmat": cmat,
        "wmix": wmix, "wglu": wglu, "wrouter": wrouter, "wdense": wdense, "wmoe": wmoe,
    }
    arrays = {k: np.ascontiguousarray(v, dtype=f32) for k, v in arrays.items()}

    nc = bacc.Bacc("TRN2", target_bir_lowering=False, num_devices=1)
    aps = [nc.dram_tensor(k, v.shape, F32, kind="ExternalInput").ap() for k, v in arrays.items()]
    out = nc.dram_tensor("y_out", (P, TT, D), F32, kind="ExternalOutput").ap()
    encoder(nc, *aps, out)
    got = run_bass_kernel_spmd(nc, [arrays], core_ids=[0]).results[0]["y_out"]
    return np.ascontiguousarray(got.transpose(1, 0, 2)).reshape(1, SEQ, D)
```

```python
import math
from contextlib import ExitStack

import numpy as np

import concourse.bass as bass
from concourse import mybir

ALU = mybir.AluOpType
ACT = mybir.ActivationFunctionType
F32 = mybir.dt.float32
F32R = mybir.dt.float32r
I32 = mybir.dt.int32
AX = mybir.AxisListType

P = 128
D = 1024
KT = D // P
SEQ = 256
TT = SEQ // P
DEPTH = 2
SW = 512
FT = SW // P
GROUP, STATE = 16, 64
NG = SW // GROUP
GP = NG // 2
ST = GP * 2
HEADS, HD = 4, 64
DFF, DFF_E, NE = 2752, 3584, 8
HC = 2 * P
NC_D = -(-DFF // HC)
NC_E = DFF_E // HC
PIECE = 4 * 2 * HC
RING = 6
AHEAD = 4
SKIP = 3
CAP = P
EPS = 1e-6
ROUND = 1.5 * 2.0 ** 23
INV2PI = 1.0 / (2.0 * math.pi)
TWOPI = 6.283185
GELU_C = math.sqrt(2.0 / math.pi)
LINIT = [0.8 - 0.6 * math.exp(-0.3 * i) for i in range(DEPTH)]
SLOPES = [2.0 ** (-8.0 * (h + 1) / HEADS) for h in range(HEADS)]

C_ID, C_ONE, C_TRI, C_DIST, C_T, C_SLOT, C_E8 = 0, 128, 256, 384, 896, 1152, 1280
C_N = 1296
Q_GMIX, Q_GFFN, Q_D, Q_BGLU, Q_GSSM, Q_GSUB, Q_LRE, Q_LIM, Q_LS, Q_LQ, Q_BR = 0, 8, 16, 20, 24, 28, 29, 61, 93, 125, 381
Q_N = Q_BR + NE

UNITS = ([("norm", "D"), ("norm", "A")] * 2 + [("zu", "A")] * 2 + [("zqkv", "A")] * 6
         + [("head", "D"), ("head", "D"), ("head", "A"), ("head", "A")] * HEADS
         + [("oss", "A")] * 2 + [("out", "D")] * 4 + [("fnorm", "D"), ("fnorm", "A")] * 2)
UL = len(UNITS)
FIRST = {}
for _i, (_s, _) in enumerate(UNITS):
    FIRST.setdefault(_s, _i)
RING0, RINGN = 4, 4
SCATTER = (4, 5, 7, 4)


def unit(l, stage, k=0):
    return l * UL + FIRST[stage] + k


def emptied(u):
    who = UNITS[u % UL][1]
    return who, (u // UL) * sum(w == who for _, w in UNITS) + sum(w == who for _, w in UNITS[:u % UL + 1])


S_MAP, S_TURN, S_OUT = 0, 2, 3


def head_start(h):
    return 8 + 5 * h


def bank(u):
    return RING0 + u % RINGN


def pieces_before(m):
    return 3 * NC_D + 3 * NC_E * m


def encoder(nc, x, consts, rows, params, bmat, cmat, wmix, wglu, wrouter, wffn, out):
    with ExitStack() as ctx:
        scope = [ctx]

        def sb(name, shape, dt=F32):
            return scope[0].enter_context(nc.sbuf_tensor(name, shape, dt))

        def sem(name):
            return ctx.enter_context(nc.semaphore(name))

        ps = ctx.enter_context(nc.psum_tensor("ps", [P, 8, 512], F32))

        X = sb("X", [P, TT, D])
        hn = sb("hn", [P, TT, D])
        hT = sb("hT", [P, KT, SEQ])
        raw = sb("raw", [P, RING, PIECE])
        cst = sb("cst", [P, C_N])
        par = sb("par", [P, DEPTH, Q_N])
        wr = sb("wr", [P, KT, NE])
        rt = sb("rt", [P, 8, TT, NE])
        cnt = sb("cnt", [1, NE], I32)
        col = sb("col", [P, 96])

        scope[0] = ExitStack()
        wh = sb("wh", [P, RING, PIECE], F32R)
        wl = sb("wl", [P, RING, PIECE], F32R)
        xh = sb("xh", [P, KT, SEQ], F32R)
        xl = sb("xl", [P, KT, SEQ], F32R)
        hidh = sb("hidh", [P, 2, SEQ], F32R)
        hidl = sb("hidl", [P, 2, SEQ], F32R)
        hv = sb("hv", [P, 2, HC])
        pick = sb("pick", [P, 2, TT, CAP])
        wT = sb("wT", [P, SEQ])
        ybuf = sb("ybuf", [P, D])
        scope[0].close()

        scope[0] = ctx
        mixw = sb("mixw", [P, 2, KT, 512])
        bw = sb("bw", [P, FT, 2, 2, P])
        small = sb("small", [P, 16, ST])
        cw = sb("cw", [P, 2, ST, 32])
        work = sb("work", [P, 28 * SEQ])

        def part(at, *shape):
            names = "abcd"[:len(shape)]
            sizes = dict(zip(names, shape))
            flat = work[:, at * SEQ:at * SEQ + math.prod(shape) * SEQ]
            return flat.rearrange(f"p ({' '.join(names)} t) -> p {' '.join(names)} t", **sizes)

        phase = part(0, 2)
        rnd = part(2, 2)
        frac = part(4, 2)
        trig = part(6, 2, 3)
        ri1 = part(12, 2)
        ri2 = part(14, 2)
        st = part(16, 2, 2)
        ro = part(20, 2, 2, 2)
        S = hn[:, 0].rearrange("p (m q t) -> p m q t", m=2, q=TT)
        A = hn[:, 1].rearrange("p (h q t) -> p h q t", h=2, q=TT)
        AT = hT[:, 0:4].rearrange("p (h k) t -> p h k t", h=2)
        osq = hT[:, 4:8].rearrange("p (k a) t -> p k a t", k=2)
        uT = sb("uT", [P, FT, SEQ])
        qT = sb("qT", [P, HEADS, SEQ])
        kT = sb("kT", [P, HEADS, SEQ])
        v = sb("v", [P, TT, 512])
        cat = sb("cat", [P, KT, SEQ])
        yt = sb("yt", [P, FT, SEQ])
        yq = sb("yq", [P, FT, SEQ])
        th = sb("th", [P, FT, SEQ])
        sd = sb("sd", [P, 3, 512])
        craw = cat[:].rearrange("p (r a) (b n) -> p r (a b) n", r=2, n=32)
        ctmp = yt[:].rearrange("p a (b n) -> p (a b) n", n=32)

        ident = cst[:, C_ID:C_ID + P]
        ones = cst[:, C_ONE:C_ONE + P]

        names = """in_x in_cst in_par in_b in_c in_glu in_wr out_done
            unit_done emptied_act emptied_dve act_chain dve_chain pool_chain
            sumsq rstd hn_ready param_load small_act small_dve small_sin cw_ready
            phase_ready frac_ready trig_ready bu_ready bu_read ri_ready scanned rotated c_done y_read
            gin gtanh g_ready glu_done glu_tanh gss_done gss_root q_ready qs_ready  score_ready exp_done att_ready sqo rms_o rms_y cat_ready
            hi_done lo_done piece_done xh_done xl_done
            silu_done hv_ready turned hid_hi hid_lo dense_added lg_done routed_exp ex_done picked weighed gathered
            wt_done wt_ready acc_act acc_dve scattered added mixer_done gain_in sel_ready pos_done tables_ready
            xh_ready final_ready fin_out lamb_in lamb_ex col_ready""".split()
        s = {n: sem(n) for n in names}
        mix_full = [sem(f"mix_full{i}") for i in range(2)]
        raw_full = [sem(f"raw_full{i}") for i in range(RING)]

        block = ctx.enter_context(nc.Block())

        def chunk(l, k):
            return 7 * l + k

        def last_use(c):
            stage, k = [("zu", 1), ("zqkv", 1), ("zqkv", 3), ("zqkv", 5), None, ("out", 1), ("out", 3)][c % 7]
            return unit(c // 7, stage, k)

        def mix_wait(eng, c):
            eng.wait_ge(mix_full[c % 2], 16 * (c // 2 + 1))

        class Stack:

            def __init__(self, m):
                self.moe, self.n = m is not None, NC_D if m is None else NC_E
                self.shift = 0 if self.moe else SKIP
                self.m = 0 if m is None else m
                self.q0, self.c0, self.k0 = (3 * NC_D, NC_D, (3 * NC_D + SKIP) // RING) if self.moe else (0, 0, 0)

            def slot(self, j):
                return (j + self.shift) % RING

            def piece(self, j, g):
                return self.m * (3 * NC_E) + g * RING + (self.q0 + j)

            def chunk(self, c, g):
                return self.m * NC_E + g * 2 + (self.c0 + c)

            def loads(self, j, g):
                turns = self.m * (3 * NC_E // RING) + g + (self.k0 + (j + self.shift) // RING)
                return turns * 16 + (0 if self.slot(j) < SKIP else 16)

            def walk(self, eng, step):
                order = [("A", 0), ("B", 0)]
                for c in range(1, self.n):
                    order += [("A", c), ("B", c), ("D", c - 1)]
                order.append(("D", self.n - 1))
                turns = (self.n - 1) // 2
                for j in range(8):
                    step(j, 0, *order[j])
                peeled = 0 if self.moe else 1
                with eng.Fori(1, turns - peeled) as g:
                    for j in range(2, 8):
                        step(j, g, *order[j])
                for j in range(2, 8) if peeled else ():
                    step(j, turns - 1, *order[j])
                for j in range(2 + 6 * turns, 3 * self.n):
                    step(j, 0, *order[j])

        def at_least(eng, what, n):
            if not isinstance(n, int) or n > 0:
                eng.wait_ge(s[what], n)

        @block.sync
        def _(sp):
            sp.dma_start(X[:], x).then_inc(s["in_x"], 16)
            sp.dma_start(par[:], params).then_inc(s["in_par"], 16)
            sp.dma_start(cst[:], consts).then_inc(s["in_cst"], 16)

            def mix(l, k):
                c = chunk(l, k)
                if k == 6:
                    sp.wait_ge(s["glu_done"], 2 * (l + 1))
                elif c >= 2 and k != 0:
                    sp.wait_ge(s["unit_done"], last_use(c - 2) + 1)
                if k == 4:
                    sp.dma_start(mixw[:, c % 2, 0:FT], wglu[l]).then_inc(mix_full[c % 2], 16)
                else:
                    sp.dma_start(mixw[:, c % 2], wmix[l, k - (k > 4)]).then_inc(mix_full[c % 2], 16)

            def load(slot, index, free):
                if free is not None:
                    sp.wait_ge(s["lo_done"], free)
                src = wffn[index] if isinstance(index, int) else wffn[bass.ds(index, 1)].rearrange("a p n -> p (a n)")
                sp.dma_start(raw[:, slot], src).then_inc(raw_full[slot], 16)

            mix(0, 0)
            mix(0, 1)
            sp.dma_start(wr[:], wrouter).then_inc(s["in_wr"], 16)
            for q in range(RING):
                load((q + SKIP) % RING, q, None)
            for k in range(2, 7):
                mix(0, k)
            with sp.Fori(1, 3 * NC_D // RING) as g:
                for j in range(RING):
                    load((j + SKIP) % RING, RING * g + j, RING * g + (j - RING + 1))
            for q in range(3 * NC_D // RING * RING, 3 * NC_D):
                load((q + SKIP) % RING, q, q - RING + 1)
            base = 3 * NC_D
            for j in range(RING):
                load(j, base + j, base + j - RING + 1)
            sp.wait_ge(s["piece_done"], base)
            for k in range(7):
                mix(1, k)
            with sp.Fori(1, NE * 3 * NC_E // RING) as g:
                for j in range(RING):
                    load(j, RING * g + (base + j), RING * g + (base + j - RING + 1))
            sp.wait_ge(s["tables_ready"], 1)
            m = sp.alloc_register("sp_pass")
            sp.reg_mov(m, NE)
            with sp.Fori(0, NE) as e:
                c = sp.value_load(cnt[0:1, bass.ds(e, 1)], min_val=0, max_val=SEQ)
                with sp.If(c > CAP):
                    n = sp.snap(m, min_val=NE, max_val=2 * NE)
                    with sp.Fori(0, 3 * NC_E // RING) as g:
                        for j in range(RING):
                            load(j, 3 * NC_E * e + RING * g + (base + j),
                                 3 * NC_E * n + RING * g + (base + j - RING + 1))
                    sp.reg_add(m, m, 1)
            sp.wait_ge(s["final_ready"], 1)
            sp.dma_start(out, hn[:]).then_inc(s["out_done"], 16)
            sp.wait_ge(s["out_done"], 16)

        @block.gpsimd
        def _(pool):
            for l in range(DEPTH):
                if l:
                    pool.wait_ge(s["piece_done"], 3 * NC_D)
                pool.dma_start(bw[:], bmat[l]).then_inc(s["in_b"], 16)
                pool.dma_start(craw[:], cmat[l]).then_inc(s["in_c"], 16)
                for i in range(ST):
                    n = ST * l + i
                    b = i % 2
                    pool.wait_ge(s["scanned"], n + 1)
                    if n >= 2:
                        pool.wait_ge(s["c_done"], n - 1)
                    nc.gpsimd.tensor_tensor(ro[:, b, 0], st[:, b], trig[:, b, 0:1, :].to_broadcast([P, 2, SEQ]),
                                            ALU.mult)
                    nc.gpsimd.tensor_tensor(ro[:, b, 1], st[:, b, ::-1, :], trig[:, b, 2:0:-1, :],
                                            ALU.mult).then_inc(s["rotated"], 1)
            pool.wait_ge(s["mixer_done"], 1)
            pool.dma_start(ybuf[:], rows[:, 0:D]).then_inc(s["gain_in"], 16)
            pool.wait_ge(s["xh_ready"], 1)
            pool.dma_start(ybuf[:], rows[:, D:2 * D]).then_inc(s["gain_in"], 16)

        @block.scalar
        def _(act):
            chain = [0]

            def link(ins):
                chain[0] += 1
                ins.then_inc(s["act_chain"], 1)
                act.wait_ge(s["act_chain"], chain[0])

            def full(u):
                act.wait_ge(s["unit_done"], u + 1)

            def norm_squares(m):
                for t in range(TT):
                    ins = nc.scalar.activation(hn[:, t], X[:, t], ACT.Square, accum_out=col[:, 2 * t:2 * t + 1])
                ins.then_inc(s["sumsq"], 1)
                act.wait_ge(s["rstd"], 2 * m + 1)
                nc.scalar.activation(col[:, 8:10], col[:, 4:6], ACT.Sqrt).then_inc(s["small_act"], 1)

            def norm_empty(l, stage, gain):
                for k in (1, 3):
                    full(unit(l, stage, k))
                    for j in range(2):
                        f = 2 * k + j
                        ins = nc.scalar.activation(hT[:, f, :], ps[:, bank(unit(l, stage, k)), j * 256:j * 256 + 256],
                                                   ACT.Copy, scale=par[:, l, gain + f:gain + f + 1])
                    ins.then_inc(s["emptied_act"], 1)

            def phases(l, i):
                n = ST * l + i
                act.wait_ge(s["small_dve"], 4 * l + 4)
                if n:
                    act.wait_ge(s["frac_ready"], n)
                nc.scalar.activation(phase[:, 0], cst[:, C_T:C_T + SEQ], ACT.Copy, scale=small[:, 4, i:i + 1])
                link(nc.scalar.activation(phase[:, 1], cst[:, C_T:C_T + SEQ], ACT.Identity, bias=col[:, 17:18],
                                          scale=small[:, 4, i:i + 1]))
                nc.scalar.activation(rnd[:], phase[:], ACT.Copy, bias=ROUND).then_inc(s["phase_ready"], 1)

            def trigs(l, i):
                n = ST * l + i
                act.wait_ge(s["frac_ready"], n + 1)
                if n >= 2:
                    act.wait_ge(s["rotated"], n - 1)
                nc.scalar.activation(trig[:, i % 2, 0], frac[:, 1], ACT.Sin, scale=-TWOPI)
                nc.scalar.activation(trig[:, i % 2, 1], frac[:, 0], ACT.Sin, scale=-TWOPI)
                nc.scalar.activation(trig[:, i % 2, 2], frac[:, 0], ACT.Sin, scale=TWOPI).then_inc(s["trig_ready"], 1)

            def gelu_tanh(l, ft):
                act.wait_ge(s["gin"], FT * l + ft + 1)
                nc.scalar.activation(th[:, ft], th[:, ft], ACT.Tanh, scale=GELU_C).then_inc(s["gtanh"], 1)

            def attention(l, h, at):
                if at == 1:
                    for m in range(2):
                        act.wait_ge(s["score_ready"], 2 * (HEADS * l + h) + m + 1)
                        for q in range(TT):
                            c = 4 * (h % 2) + 2 * m + q
                            ins = nc.scalar.activation(S[:, m, q], S[:, m, q], ACT.Exp, bias=col[:, 64 + c:65 + c],
                                                       accum_out=col[:, 72 + c:73 + c])
                    ins.then_inc(s["exp_done"], 1)
                elif at == 3:
                    u = unit(l, "head", 4 * h + S_TURN)
                    full(u)
                    nc.scalar.activation(AT[:, h % 2], ps[:, bank(u)].rearrange("p (k t) -> p k t", k=TT),
                                         ACT.Copy).then_inc(s["emptied_act"], 1)
                elif at == 4:
                    u = unit(l, "head", 4 * h + S_OUT)
                    full(u)
                    nc.scalar.activation(cat[:, FT + h], ps[:, bank(u), 0:SEQ], ACT.Copy)
                    nc.scalar.activation(osq[:, h // 2, h % 2], ps[:, bank(u), 0:SEQ],
                                         ACT.Square).then_inc(s["emptied_act"], 1)

            def upper(stack, j, g):
                q, slot = stack.piece(j, g), stack.slot(j)
                act.wait_ge(raw_full[slot], stack.loads(j, g))
                at_least(act, "piece_done", q - (RING - 1))
                nc.scalar.activation(wh[:, slot], raw[:, slot], ACT.Copy).then_inc(s["hi_done"], 1)

            def stream(stack, nt, more, middle=None):
                w = nt * P

                def hidden_upper(c, g):
                    act.wait_ge(s["turned"], stack.chunk(c, g) + 1)
                    nc.scalar.activation(hidh[:, :, 0:w], ps[:, 6, 0:2 * w].rearrange("p (a t) -> p a t", a=2),
                                         ACT.Copy).then_inc(s["hid_hi"], 1)

                def step(j, g, kind, c):
                    if more or not isinstance(g, int) or j + RING * g + AHEAD < 3 * stack.n:
                        upper(stack, j + AHEAD, g)
                    if kind == "A" and c:
                        hidden_upper(c - 1, g)
                    if kind == "B":
                        k = stack.chunk(c, g)
                        act.wait_ge(s["piece_done"], stack.piece(j, g) + 1)
                        at_least(act, "turned", k)
                        b = c % 2 if nt == 1 else 0
                        nc.scalar.activation(hv[:, 0:nt], ps[:, b:b + nt, 0:HC], ACT.Silu).then_inc(s["silu_done"], 1)
                    if j == 3 * stack.n - 1:
                        hidden_upper(c, g)
                        if middle:
                            middle()
                stack.walk(act, step)

            for l in range(DEPTH):
                if l == 0:
                    act.wait_ge(s["in_par"], 16)
                else:
                    act.wait_ge(s["dense_added"], 1)
                pr = par[:, l]
                nc.scalar.activation(small[:, 0], pr[:, Q_LS:Q_LS + ST], ACT.Exp).then_inc(s["small_act"], 1)
                act.wait_ge(s["small_dve"], 4 * l + 1)
                nc.scalar.activation(small[:, 3], small[:, 1], ACT.Exp)
                nc.scalar.activation(col[:, 12:14], col[:, 10:12], ACT.Exp).then_inc(s["small_act"], 1)
                act.wait_ge(s["small_dve"], 4 * l + 2)
                nc.scalar.activation(small[:, 5:7], small[:, 7:9], ACT.Sin, scale=-TWOPI).then_inc(s["small_act"], 1)

                if l == 0:
                    act.wait_ge(s["in_x"], 16)
                else:
                    act.wait_ge(s["dense_added"], 1)
                norm_squares(2 * l)
                norm_empty(l, "norm", Q_GMIX)
                for k in range(2):
                    u = unit(l, "zu", k)
                    full(u)
                    nc.scalar.activation(uT[:, 2 * k:2 * k + 2, :], ps[:, bank(u)].rearrange("p (a t) -> p a t", a=2),
                                         ACT.Copy).then_inc(s["emptied_act"], 1)
                phases(l, 0)
                trigs(l, 0)
                for i in range(ST):
                    if i + 1 < ST:
                        phases(l, i + 1)
                        trigs(l, i + 1)
                    if 1 <= i <= 6:
                        k = i - 1
                        u = unit(l, "zqkv", k)
                        full(u)
                        pb = ps[:, bank(u)]
                        if k < 4:
                            dst = (qT, kT)[k // 2][:, 2 * (k % 2):2 * (k % 2) + 2, :]
                            nc.scalar.activation(dst, pb.rearrange("p (a t) -> p a t", a=2), ACT.Copy,
                                                 scale=(HD ** -0.5 if k < 2 else 1.0)).then_inc(s["emptied_act"], 1)
                        else:
                            nc.scalar.activation(v[:, k - 4], pb, ACT.Copy).then_inc(s["emptied_act"], 1)
                    for h in range(HEADS):
                        attention(l, h, i - head_start(h))
                    if i % 8 == 1 and i > 1:
                        gelu_tanh(l, i // 8 - 1)
                for k in range(2):
                    u = unit(l, "oss", k)
                    full(u)
                    nc.scalar.activation(sd[:, k], ps[:, bank(u)], ACT.Sqrt, bias=col[:, 18:19],
                                         scale=1.0 / (2 * HD)).then_inc(s["emptied_act"], 1)
                gelu_tanh(l, FT - 1)
                for k in range(2):
                    act.wait_ge(s["glu_done"], 2 * l + k + 1)
                    for j in range(2):
                        f = 2 * k + j
                        ins = nc.scalar.activation(th[:, f], ps[:, k, j * 256:j * 256 + 256], ACT.Tanh,
                                                   bias=col[:, 20 + f:21 + f], scale=0.25)
                    ins.then_inc(s["glu_tanh"], 1)
                act.wait_ge(s["gss_done"], l + 1)
                nc.scalar.activation(sd[:, 2, 0:SEQ], ps[:, 2, 0:SEQ], ACT.Sqrt, bias=col[:, 19:20],
                                     scale=1.0 / SW).then_inc(s["gss_root"], 1)

                act.wait_ge(s["emptied_dve"], emptied(unit(l, "out", 3))[1])
                stack = Stack(None if l == 0 else 0)
                norm_squares(2 * l + 1)
                upper(stack, 0, 0)
                upper(stack, 1, 0)
                norm_empty(l, "fnorm", Q_GFFN)
                if l == 0:
                    act.wait_ge(s["emptied_dve"], emptied(unit(l, "fnorm", 2))[1])
                    act.wait_ge(s["emptied_act"], emptied(unit(l, "fnorm", 3))[1])
                    nc.scalar.activation(xh[:], hT[:], ACT.Copy).then_inc(s["xh_done"], 1)
                for j in range(2, AHEAD):
                    upper(stack, j, 0)
                if l == 0:
                    stream(stack, TT, False)

            act.wait_ge(s["routed_exp"], 1)
            nc.scalar.activation(col[:, 44:46], col[:, 40:42], ACT.Exp).then_inc(s["ex_done"], 1)

            def gather(m):
                act.wait_ge(s["gathered"], m + 1)
                nc.scalar.activation(xh[:, :, 0:CAP], ps[:, 4:6].rearrange("p b (a t) -> p (b a) t", a=4),
                                     ACT.Copy).then_inc(s["xh_done"], 1)

            def expert(m, more):
                stack = Stack(m)

                def middle():
                    act.wait_ge(s["wt_done"], m + 1)
                    nc.scalar.activation(wT[:], ps[:, 7, 0:SEQ], ACT.Copy).then_inc(s["wt_ready"], 1)
                    if more:
                        gather(m + 1)
                stream(stack, 1, more, middle)
                act.wait_ge(s["piece_done"], stack.piece(3 * NC_E, 0))
                nc.scalar.activation(ybuf[:, 0:512], ps[:, 2], ACT.Copy).then_inc(s["acc_act"], 1)

            gather(0)
            expert(0, True)
            with act.Fori(1, NE - 1) as e:
                expert(e, True)
            expert(NE - 1, False)
            act.wait_ge(s["tables_ready"], 1)
            m = act.alloc_register("act_pass")
            act.reg_mov(m, NE)
            with act.Fori(0, NE) as e:
                c = act.value_load(cnt[0:1, bass.ds(e, 1)], min_val=0, max_val=SEQ)
                with act.If(c > CAP):
                    n = act.snap(m, min_val=NE, max_val=2 * NE)
                    for j in range(AHEAD):
                        upper(Stack(n), j, 0)
                    gather(n)
                    expert(n, False)
                    act.reg_add(m, m, 1)
            act.wait_ge(s["xh_ready"], 1)
            norm_squares(2 * DEPTH)

        @block.vector
        def _(dve):
            chain = [0]

            def link(ins):
                chain[0] += 1
                ins.then_inc(s["dve_chain"], 1)
                dve.wait_ge(s["dve_chain"], chain[0])

            def full(u):
                dve.wait_ge(s["unit_done"], u + 1)

            ts, tt, stt = nc.vector.tensor_scalar, nc.vector.tensor_tensor, nc.vector.scalar_tensor_tensor

            link(nc.vector.memset(col[:, 17:18], 0.25))
            link(nc.vector.memset(col[:, 18:19], EPS))
            link(nc.vector.memset(col[:, 19:20], 16 * EPS))

            small_acts = [0]

            def small_act():
                small_acts[0] += 1
                dve.wait_ge(s["small_act"], small_acts[0])

            def norm_scale(m):
                dve.wait_ge(s["sumsq"], m + 1)
                ts(col[:, 4:6], col[:, 0:4:2], 1.0 / D, EPS, ALU.mult, ALU.add).then_inc(s["rstd"], 2)
                small_act()
                link(nc.vector.reciprocal(col[:, 6:8], col[:, 8:10]))
                for t in range(TT):
                    ins = ts(hn[:, t], X[:, t], col[:, 6 + t:7 + t], None, ALU.mult)
                ins.then_inc(s["hn_ready"], 1)

            def norm_empty(l, stage, gain):
                for k in (0, 2):
                    u = unit(l, stage, k)
                    full(u)
                    for j in range(2):
                        f = 2 * k + j
                        ins = ts(hT[:, f, :], ps[:, bank(u), j * 256:j * 256 + 256],
                                 par[:, l, gain + f:gain + f + 1], None, ALU.mult)
                    ins.then_inc(s["emptied_dve"], 1)

            def wrap(dst, src, tmp):
                link(ts(tmp, src, ROUND, None, ALU.add))
                link(stt(dst, tmp, ROUND, src, ALU.subtract, ALU.subtract))

            def scalars(l):
                pr = par[:, l]
                sm = small
                small_act()
                link(tt(sm[:, 1], pr[:, Q_LRE:Q_LRE + ST], sm[:, 0], ALU.mult))
                link(tt(th[:, 0, 0:2 * HD].rearrange("p (a d) -> p a d", a=2),
                        pr[:, Q_LQ:Q_LQ + 4 * HD].rearrange("p (a b d) -> p a b d", a=2, b=2)[:, :, 0],
                        pr[:, Q_LQ:Q_LQ + 4 * HD].rearrange("p (a b d) -> p a b d", a=2, b=2)[:, :, 1], ALU.mult))
                nc.vector.reduce_sum(col[:, 10:12], th[:, 0, 0:2 * HD].rearrange("p (a d) -> p a d", a=2),
                                     axis=AX.X).then_inc(s["small_dve"], 1)
                link(tt(sm[:, 2], pr[:, Q_LIM:Q_LIM + ST], sm[:, 0], ALU.mult))
                link(ts(sm[:, 2], sm[:, 2], INV2PI, None, ALU.mult))
                wrap(sm[:, 7], sm[:, 2], sm[:, 9])
                link(ts(sm[:, 4], sm[:, 7], -1.0, None, ALU.mult))
                link(ts(sm[:, 10], sm[:, 4], 0.25, None, ALU.add))
                link(ts(sm[:, 9], sm[:, 10], ROUND, None, ALU.add))
                stt(sm[:, 8], sm[:, 9], ROUND, sm[:, 10], ALU.subtract, ALU.subtract).then_inc(s["small_dve"], 1)
                small_act()
                link(ts(col[:, 14:15], col[:, 13:14], col[:, 12:13], -LINIT[l], ALU.subtract, ALU.add))
                link(ts(col[:, 15:16], pr[:, Q_GSUB:Q_GSUB + 1], 1.0 - LINIT[l], None, ALU.mult))
                link(ts(col[:, 20:24], pr[:, Q_BGLU:Q_BGLU + 4], 0.5, None, ALU.mult))
                small_act()
                lre, lim = pr[:, Q_LRE:Q_LRE + ST], pr[:, Q_LIM:Q_LIM + ST]
                link(tt(sm[:, 9], sm[:, 3], sm[:, 6], ALU.mult))
                link(ts(sm[:, 9], sm[:, 9], -1.0, None, ALU.add))
                link(tt(sm[:, 10], sm[:, 3], sm[:, 5], ALU.mult))
                link(tt(sm[:, 11], lre, lre, ALU.mult))
                link(tt(sm[:, 12], lim, lim, ALU.mult))
                link(tt(sm[:, 11], sm[:, 11], sm[:, 12], ALU.add))
                link(nc.vector.reciprocal(sm[:, 11], sm[:, 11]))
                link(tt(sm[:, 12], sm[:, 9], lre, ALU.mult))
                link(tt(sm[:, 13], sm[:, 10], lim, ALU.mult))
                link(tt(sm[:, 12], sm[:, 12], sm[:, 13], ALU.add))
                link(tt(sm[:, 14], sm[:, 12], sm[:, 11], ALU.mult))
                link(tt(sm[:, 12], sm[:, 10], lre, ALU.mult))
                link(tt(sm[:, 13], sm[:, 9], lim, ALU.mult))
                link(tt(sm[:, 12], sm[:, 12], sm[:, 13], ALU.subtract))
                link(tt(sm[:, 15], sm[:, 12], sm[:, 11], ALU.mult))
                ts(sm[:, 0], sm[:, 15], -1.0, None, ALU.mult).then_inc(s["small_dve"], 2)

            def fold_c(l):
                sm = small

                def b(r):
                    return sm[:, r, :].rearrange("p (t a) -> p t a", a=1).to_broadcast([P, ST, 32])
                dve.wait_ge(s["small_dve"], 4 * l + 4)
                dve.wait_ge(s["in_c"], 16 * (l + 1))
                link(tt(cw[:, 0], craw[:, 0], b(14), ALU.mult))
                link(tt(ctmp[:], craw[:, 1], b(15), ALU.mult))
                link(tt(cw[:, 0], cw[:, 0], ctmp[:], ALU.subtract))
                link(tt(cw[:, 1], craw[:, 0], b(0), ALU.mult))
                link(tt(ctmp[:], craw[:, 1], b(14), ALU.mult))
                tt(cw[:, 1], cw[:, 1], ctmp[:], ALU.subtract).then_inc(s["cw_ready"], 1)

            def fracs(l, i):
                n = ST * l + i
                dve.wait_ge(s["phase_ready"], n + 1)
                if n:
                    dve.wait_ge(s["trig_ready"], n)
                stt(frac[:], rnd[:], ROUND, phase[:], ALU.subtract, ALU.subtract).then_inc(s["frac_ready"], 1)

            def gelu_in(l, ft):
                dve.wait_ge(s["c_done"], ST * l + 8 * (ft + 1))
                y = yt[:, ft]
                stt(y, uT[:, ft], par[:, l, Q_D + ft:Q_D + ft + 1], ps[:, 2 + ft % 2, 0:SEQ],
                    ALU.mult, ALU.add).then_inc(s["y_read"], 1)
                dve.wait_ge(s["y_read"], FT * l + ft + 1)
                link(tt(th[:, ft], y, y, ALU.mult))
                link(ts(th[:, ft], th[:, ft], 0.044715, 1.0, ALU.mult, ALU.add))
                tt(th[:, ft], th[:, ft], y, ALU.mult).then_inc(s["gin"], 1)

            def gelu_out(l, ft):
                dve.wait_ge(s["gtanh"], FT * l + ft + 1)
                stt(yq[:, ft], th[:, ft], 1.0, yt[:, ft], ALU.add, ALU.mult).then_inc(s["g_ready"], 1)

            def rotate_in(l, i):
                n = ST * l + i
                b = i % 2
                dve.wait_ge(s["trig_ready"], n + 1)
                dve.wait_ge(s["bu_ready"], n + 1)
                if n:
                    dve.wait_ge(s["scanned"], n)
                bu = ps[:, b].rearrange("p (r t) -> p r t", r=2)
                tt(ri1[:], bu, trig[:, b, 0:1, :].to_broadcast([P, 2, SEQ]), ALU.mult)
                tt(ri2[:], bu[:, ::-1, :], trig[:, b, 1:3, :], ALU.mult).then_inc(s["bu_read"], 1)

            def add_in(l, i):
                dve.wait_ge(s["bu_read"], ST * l + i + 1)
                tt(ri1[:], ri1[:], ri2[:], ALU.add).then_inc(s["ri_ready"], 1)

            def scan(l, i):
                n = ST * l + i
                b = i % 2
                dve.wait_ge(s["ri_ready"], n + 1)
                if n >= 2:
                    dve.wait_ge(s["rotated"], n - 1)
                decay = small[:, 3, i:i + 1].to_broadcast([P, SEQ])
                for r in range(2):
                    ins = nc.vector.tensor_tensor_scan(st[:, b, r], decay, ri1[:, r], 0.0, ALU.mult, ALU.add)
                ins.then_inc(s["scanned"], 1)

            def score(l, h, m):
                u = unit(l, "head", 4 * h + S_MAP + m)
                full(u)
                if HEADS * l + h:
                    dve.wait_ge(s["att_ready"], HEADS * l + h)
                dist = cst[:, C_DIST:C_DIST + TT * SEQ].rearrange("p (a t) -> p a t", a=TT)
                stt(S[:, m], dist, -SLOPES[h], ps[:, bank(u)].rearrange("p (a t) -> p a t", a=TT),
                    ALU.mult, ALU.add).then_inc(s["emptied_dve"], 1)
                dve.wait_ge(s["emptied_dve"], emptied(u)[1])
                c = 64 + 4 * (h % 2) + 2 * m
                link(nc.vector.reduce_max(col[:, 34:36], S[:, m], axis=AX.X))
                ts(col[:, c:c + 2], col[:, 34:36], -1.0, None, ALU.mult).then_inc(s["score_ready"], 1)

            def attend(l, h):
                b = h % 2
                dve.wait_ge(s["exp_done"], HEADS * l + h + 1)
                if h >= 2:
                    dve.wait_ge(s["unit_done"], unit(l, "head", 4 * (h - 2) + S_TURN) + 1)
                link(nc.vector.reciprocal(col[:, 80:84], col[:, 72 + 4 * b:76 + 4 * b]))
                link(ts(col[:, 82:84], col[:, 82:84], col[:, 14:15], None, ALU.mult))
                for q in range(TT):
                    ins = ts(A[:, b, q], S[:, 1, q], col[:, 82 + q:83 + q], None, ALU.mult)
                link(ins)
                for q in range(TT):
                    ins = stt(A[:, b, q], S[:, 0, q], col[:, 80 + q:81 + q], A[:, b, q], ALU.mult, ALU.add)
                ins.then_inc(s["att_ready"], 1)

            def lower(stack, j, g):
                dve.wait_ge(s["hi_done"], stack.piece(j, g) + 1)
                slot = stack.slot(j)
                tt(wl[:, slot], raw[:, slot], wh[:, slot].bitcast(F32), ALU.subtract).then_inc(s["lo_done"], 1)

            def stream(stack, nt, more, early=None, middle=None):
                w = nt * P

                def hidden_lower(c, g):
                    dve.wait_ge(s["hid_hi"], stack.chunk(c, g) + 1)
                    tt(hidl[:, :, 0:w], ps[:, 6, 0:2 * w].rearrange("p (a t) -> p a t", a=2),
                       hidh[:, :, 0:w].bitcast(F32), ALU.subtract).then_inc(s["hid_lo"], 1)

                def step(j, g, kind, c):
                    if more or not isinstance(g, int) or j + RING * g + AHEAD < 3 * stack.n:
                        lower(stack, j + AHEAD, g)
                    if kind == "A" and c:
                        hidden_lower(c - 1, g)
                    if kind == "B":
                        k = stack.chunk(c, g)
                        dve.wait_ge(s["silu_done"], k + 1)
                        b = c % 2 if nt == 1 else 0
                        tt(hv[:, 0:nt], hv[:, 0:nt], ps[:, b:b + nt, HC:2 * HC], ALU.mult).then_inc(s["hv_ready"], 1)
                    if j == 1 and early:
                        early()
                    if j == 3 * stack.n - 1:
                        hidden_lower(c, g)
                        if middle:
                            middle()
                stack.walk(dve, step)

            for l in range(DEPTH):
                if l == 0:
                    dve.wait_ge(s["in_par"], 16)
                    dve.wait_ge(s["in_x"], 16)
                scalars(l)
                norm_scale(2 * l)
                fold_c(l)
                norm_empty(l, "norm", Q_GMIX)
                fracs(l, 0)
                for i in range(ST):
                    rotate_in(l, i)
                    if i + 1 < ST:
                        fracs(l, i + 1)
                    add_in(l, i)
                    for h in range(HEADS):
                        if i == head_start(h) + 1:
                            score(l, h, 0)
                            score(l, h, 1)
                        if i == head_start(h) + 2:
                            attend(l, h)
                    if i % 8 == 1 and i > 1:
                        gelu_in(l, i // 8 - 1)
                    if i % 8 == 2 and i > 2:
                        gelu_out(l, i // 8 - 1)
                    scan(l, i)
                gelu_in(l, FT - 1)
                for k in range(2):
                    dve.wait_ge(s["emptied_act"], emptied(unit(l, "oss", k))[1])
                    link(nc.vector.reciprocal(sd[:, k], sd[:, k]))
                    f = slice(FT + 2 * k, FT + 2 * k + 2)
                    ins = stt(cat[:, f], cat[:, f], col[:, 15:16], sd[:, k].rearrange("p (a t) -> p a t", a=2),
                              ALU.mult, ALU.mult)
                    if k == 0:
                        gelu_out(l, FT - 1)
                ins.then_inc(s["cat_ready"], 1)
                for k in range(2):
                    dve.wait_ge(s["glu_tanh"], 2 * l + k + 1)
                    f = slice(2 * k, 2 * k + 2)
                    link(stt(yt[:, f], th[:, f], 1.0, yq[:, f], ALU.add, ALU.mult))
                    ins = tt(th[:, f], yt[:, f], yt[:, f], ALU.mult)
                ins.then_inc(s["qs_ready"], 1)
                dve.wait_ge(s["gss_root"], l + 1)
                link(nc.vector.reciprocal(sd[:, 2, 0:SEQ], sd[:, 2, 0:SEQ]))
                for f in range(FT):
                    ins = stt(cat[:, f], yt[:, f], par[:, l, Q_GSSM + f:Q_GSSM + f + 1], sd[:, 2, 0:SEQ],
                              ALU.mult, ALU.mult)
                ins.then_inc(s["cat_ready"], 1)
                for k in range(4):
                    u = unit(l, "out", k)
                    full(u)
                    xs = X[:, k % 2, (k // 2) * 512:(k // 2) * 512 + 512]
                    tt(xs, xs, ps[:, bank(u)], ALU.add).then_inc(s["emptied_dve"], 1)
                stack = Stack(None if l == 0 else 0)
                norm_scale(2 * l + 1)
                if l:
                    nc.vector.memset(col[:, 61:62], 0.0).then_inc(s["mixer_done"], 1)
                lower(stack, 0, 0)
                norm_empty(l, "fnorm", Q_GFFN)
                if l == 0:
                    dve.wait_ge(s["emptied_dve"], emptied(unit(l, "fnorm", 2))[1])
                    dve.wait_ge(s["xh_done"], 1)
                    tt(xl[:], hT[:], xh[:].bitcast(F32), ALU.subtract).then_inc(s["xl_done"], 1)
                for j in range(1, AHEAD):
                    lower(stack, j, 0)
                if l == 0:
                    stream(stack, TT, False)
                    dve.wait_ge(s["piece_done"], 3 * NC_D)
                    for t in range(TT):
                        xs = X[:, t].rearrange("p (a n) -> p a n", a=2)
                        ins = tt(xs, xs, ps[:, 2 + 2 * t:4 + 2 * t], ALU.add)
                    ins.then_inc(s["dense_added"], 1)
                    dve.wait_ge(s["dense_added"], 1)

            dve.wait_ge(s["gain_in"], 16)
            full(unit(DEPTH - 1, "fnorm", 3))
            for t in range(TT):
                link(tt(hn[:, t], hn[:, t], ybuf[:], ALU.mult))
            dve.wait_ge(s["lg_done"], 1)
            e8 = cst[:, C_E8:C_E8 + 16].rearrange("p (a e) -> p a e", a=TT)
            lg, oh0, oh1, tmp, sel, gate = (rt[:, j] for j in range(6))

            def wide(c):
                return col[:, c:c + TT].rearrange("p (a b) -> p a b", b=1).to_broadcast([P, TT, NE])

            def largest(val, onehot):
                link(nc.vector.reduce_max(col[:, val:val + TT], lg, axis=AX.X))
                link(tt(tmp, lg, wide(val), ALU.is_equal))
                link(tt(tmp, tmp, e8, ALU.mult))
                link(nc.vector.tensor_reduce(col[:, 48:50], tmp, axis=AX.X, op=ALU.min))
                link(tt(onehot, e8, wide(48), ALU.is_equal))

            lgp = ps[:, 4, 0:TT * NE].rearrange("p (a e) -> p a e", a=TT)
            br = par[:, 0, Q_BR:Q_BR + NE].rearrange("p (a e) -> p a e", a=1).to_broadcast([P, TT, NE])
            link(tt(lg, lgp, br, ALU.add))
            largest(50, oh0)
            link(stt(lg, oh0, -3.0e38, lg, ALU.mult, ALU.add))
            largest(52, oh1)
            tt(col[:, 40:42], col[:, 52:54], col[:, 50:52], ALU.subtract).then_inc(s["routed_exp"], 1)
            tt(sel, oh0, oh1, ALU.add).then_inc(s["sel_ready"], 1)
            dve.wait_ge(s["ex_done"], 1)
            link(ts(col[:, 42:44], col[:, 44:46], 1.0, None, ALU.add))
            link(nc.vector.reciprocal(col[:, 54:56], col[:, 42:44]))
            link(tt(col[:, 56:58], col[:, 44:46], col[:, 54:56], ALU.mult))
            link(tt(gate, oh0, wide(54), ALU.mult))
            link(tt(tmp, oh1, wide(56), ALU.mult))
            link(tt(gate, gate, tmp, ALU.add))
            dve.wait_ge(s["pos_done"], 1)
            pos = ps[:, 5, 0:TT * NE].rearrange("p (a e) -> p a e", a=TT)
            link(ts(rt[:, 6], pos, 1.0, None, ALU.add))
            link(tt(rt[:, 6], rt[:, 6], sel, ALU.mult))
            link(ts(rt[:, 7], rt[:, 6], -1.0 - CAP, None, ALU.add))
            link(ts(rt[:, 6], rt[:, 6], -1.0, None, ALU.add))
            nc.vector.tensor_copy(cnt[:], ps[0:1, 5, TT * NE:TT * NE + NE]).then_inc(s["tables_ready"], 1)
            dve.wait_ge(s["tables_ready"], 1)

            def find(m, e, part, weighted):
                slot = cst[:, C_SLOT:C_SLOT + CAP]
                e = slice(e, e + 1) if isinstance(e, int) else bass.ds(e, 1)
                at_least(dve, "wt_done" if weighted else "gathered", m)
                for t in range(TT):
                    if weighted:
                        ins = ts(pick[:, 1, t], slot, rt[:, 6 + part, t, e], rt[:, 5, t, e], ALU.is_equal, ALU.mult)
                    else:
                        ins = ts(pick[:, 0, t], slot, rt[:, 6 + part, t, e], None, ALU.is_equal)
                ins.then_inc(s["weighed" if weighted else "picked"], 1)

            def gather(m):
                dve.wait_ge(s["xh_done"], m + 2)
                tt(xl[:, :, 0:CAP], ps[:, 4:6].rearrange("p b (a t) -> p (b a) t", a=4),
                   xh[:, :, 0:CAP].bitcast(F32), ALU.subtract).then_inc(s["xl_done"], 1)

            def add(m):
                for k in range(2 * TT):
                    dve.wait_ge(s["scattered"], 2 * TT * m + (k + 1))
                    xs = X[:, k // 2, (k % 2) * 512:(k % 2) * 512 + 512]
                    tt(xs, xs, ps[:, SCATTER[k]], ALU.add).then_inc(s["added"], 1)

            def expert(m, e, part, prev, more):
                def early():
                    if prev:
                        add(m - 1)
                    find(m, e, part, True)
                    if more:
                        find(m + 1, e + 1, 0, False)
                stack = Stack(m)
                stream(stack, 1, more, early, (lambda: gather(m + 1)) if more else None)
                dve.wait_ge(s["piece_done"], stack.piece(3 * NC_E, 0))
                nc.vector.tensor_copy(ybuf[:, 512:D], ps[:, 3]).then_inc(s["acc_dve"], 1)

            find(0, 0, 0, False)
            gather(0)
            expert(0, 0, 0, False, True)
            with dve.Fori(1, NE - 1) as e:
                expert(e, e, 0, True, True)
            expert(NE - 1, NE - 1, 0, True, False)
            add(NE - 1)
            m = dve.alloc_register("dve_pass")
            dve.reg_mov(m, NE)
            with dve.Fori(0, NE) as e:
                c = dve.value_load(cnt[0:1, bass.ds(e, 1)], min_val=0, max_val=SEQ)
                with dve.If(c > CAP):
                    n = dve.snap(m, min_val=NE, max_val=2 * NE)
                    for j in range(AHEAD):
                        lower(Stack(n), j, 0)
                    find(n, e, 1, False)
                    gather(n)
                    expert(n, e, 1, False, False)
                    add(n)
                    dve.reg_add(m, m, 1)

            nc.vector.memset(col[:, 60:61], 0.0).then_inc(s["xh_ready"], 1)
            norm_scale(2 * DEPTH)
            dve.wait_ge(s["hn_ready"], 2 * DEPTH + 1)
            dve.wait_ge(s["gain_in"], 32)
            for t in range(TT):
                ins = tt(hn[:, t], hn[:, t], ybuf[:], ALU.mult)
            ins.then_inc(s["final_ready"], 1)

        @block.tensor
        def _(pe):
            mm = nc.tensor.matmul

            def free(u):
                if u >= RINGN:
                    who, n = emptied(u - RINGN)
                    pe.wait_ge(s["emptied_act" if who == "A" else "emptied_dve"], n)

            def empty_wait(u):
                who, n = emptied(u)
                pe.wait_ge(s["emptied_act" if who == "A" else "emptied_dve"], n)

            def norm(l, stage, m):
                pe.wait_ge(s["hn_ready"], m + 1)
                for k in range(4):
                    u = unit(l, stage, k)
                    free(u)
                    for j in range(2):
                        for t in range(TT):
                            f = 2 * k + j
                            ins = nc.tensor.transpose(ps[:, bank(u), j * 256 + t * P:j * 256 + (t + 1) * P],
                                                      hn[:, t, f * P:(f + 1) * P], ident)
                    ins.then_inc(s["unit_done"], 1)

            def ht_ready(l, stage):
                empty_wait(unit(l, stage, 2))
                empty_wait(unit(l, stage, 3))

            def project(l, u, c, k):
                free(u)
                for j in range(2):
                    n = 2 * k + j
                    for f in range(KT):
                        ins = mm(ps[:, bank(u), j * 256:j * 256 + 256], mixw[:, c % 2, f, n * P:(n + 1) * P],
                                 hT[:, f, :], start=(f == 0), stop=(f == KT - 1))
                ins.then_inc(s["unit_done"], 1)
                return ins

            def bu(l, i):
                n = ST * l + i
                if n >= 2:
                    pe.wait_ge(s["bu_read"], n - 1)
                gp, d = i // 2, i % 2
                ft, q = gp // 4, 32 * (gp % 4)
                u = uT[q:q + 32, ft, ::-1] if d else uT[q:q + 32, ft, :]
                for r in range(2):
                    ins = mm(ps[:, i % 2, r * 256:r * 256 + 256], bw[q:q + 32, ft, d, r, :], u, start=True, stop=True,
                             tile_position=(q, 0))
                ins.then_inc(s["bu_ready"], 1)

            def outputs(l, i):
                n = ST * l + i
                gp, d = i // 2, i % 2
                ft, q = gp // 4, 32 * (gp % 4)
                if i % 8 == 0 and FT * l + ft >= 2:
                    pe.wait_ge(s["y_read"], FT * l + ft - 1)
                pe.wait_ge(s["rotated"], n + 1)
                for k in range(2):
                    for r in range(2):
                        a = ro[:, i % 2, k, r, ::-1] if d else ro[:, i % 2, k, r, :]
                        ins = mm(ps[q:q + 32, 2 + ft % 2, 0:SEQ], cw[:, r, i, :], a,
                                 start=(d == 0 and k == 0 and r == 0), stop=(d == 1 and k == 1 and r == 1),
                                 tile_position=(0, q))
                ins.then_inc(s["c_done"], 1)

            def attention(l, h, at):
                if at == 0:
                    for m in range(2):
                        u = unit(l, "head", 4 * h + S_MAP + m)
                        free(u)
                        if h == 0:
                            empty_wait(unit(l, "zqkv", 5))
                        r = slice(HD * m, HD * m + HD)
                        for q in range(TT):
                            ins = mm(ps[:, bank(u), q * 256:q * 256 + 256], qT[r, h, q * P:(q + 1) * P], kT[r, h, :],
                                     start=True, stop=True)
                        ins.then_inc(s["unit_done"], 1)
                elif at == 3:
                    u = unit(l, "head", 4 * h + S_TURN)
                    free(u)
                    pe.wait_ge(s["att_ready"], HEADS * l + h + 1)
                    for kt in range(TT):
                        for q in range(TT):
                            ins = nc.tensor.transpose(ps[:, bank(u), kt * 256 + q * P:kt * 256 + (q + 1) * P],
                                                      A[:, h % 2, q, kt * P:(kt + 1) * P], ident)
                    ins.then_inc(s["unit_done"], 1)
                elif at == 4:
                    u = unit(l, "head", 4 * h + S_OUT)
                    free(u)
                    empty_wait(unit(l, "head", 4 * h + S_TURN))
                    for kt in range(TT):
                        ins = mm(ps[:, bank(u), 0:SEQ], v[:, kt, h * P:(h + 1) * P], AT[:, h % 2, kt],
                                 start=(kt == 0), stop=(kt == TT - 1))
                    ins.then_inc(s["unit_done"], 1)

            def zqkv(l, k):
                u = unit(l, "zqkv", k)
                if k % 2 == 0:
                    mix_wait(pe, chunk(l, 1 + k // 2))
                if k < 4:
                    project(l, u, chunk(l, 1 + k // 2), k % 2)
                else:
                    free(u)
                    t = k - 4
                    for f in range(KT):
                        ins = mm(ps[:, bank(u), :], hT[:, f, t * P:(t + 1) * P], mixw[:, chunk(l, 3) % 2, f, :],
                                 start=(f == 0), stop=(f == KT - 1))
                    ins.then_inc(s["unit_done"], 1)

            def stream(stack, nt, after_b0=None, middle=None):
                halves = ((xh, wh), (xl, wh), (xh, wl))

                def turn(c, g):
                    pe.wait_ge(s["hv_ready"], stack.chunk(c, g) + 1)
                    for a in range(2):
                        for t in range(nt):
                            ins = nc.tensor.transpose(ps[:, 6, (a * nt + t) * P:(a * nt + t + 1) * P],
                                                      hv[:, t, a * P:(a + 1) * P], ident)
                    ins.then_inc(s["turned"], 1)

                def step(j, g, kind, c):
                    q, slot, k = stack.piece(j, g), stack.slot(j), stack.chunk(c, g)
                    if j == 3 * stack.n - 1:
                        turn(c, g)
                        if middle:
                            middle()
                    pe.wait_ge(s["lo_done"], q + 1)
                    if kind == "D":
                        pe.wait_ge(s["hid_lo"], k + 1)
                        first, last = j == 4 and isinstance(g, int) and g == 0, j == 3 * stack.n - 1
                        for a in range(2):
                            for t in range(nt):
                                for i, (x2, w2) in enumerate(((hidh, wh), (hidl, wh), (hidh, wl))):
                                    for n in range(2):
                                        at = a * D + n * 512
                                        ins = mm(ps[:, 2 + 2 * t + n], x2[:, a, t * P:(t + 1) * P],
                                                 w2[:, slot, at:at + 512], start=first and a == 0 and i == 0, stop=last and a == 1 and i == 2)
                        ins.then_inc(s["piece_done"], 1)
                        return
                    if kind == "A":
                        at_least(pe, "hv_ready", k if nt == TT else k - 1)
                    for t in range(nt):
                        b = t if nt == TT else c % 2
                        for f in range(4):
                            fx = f + (4 if kind == "B" else 0)
                            for i, (x2, w2) in enumerate(halves):
                                ins = mm(ps[:, b], x2[:, fx, t * P:(t + 1) * P], w2[:, slot, f * 512:(f + 1) * 512],
                                         start=(fx == 0 and i == 0), stop=(fx == KT - 1 and i == 2))
                    ins.then_inc(s["piece_done"], 1)
                    if kind == "A" and c:
                        turn(c - 1, g)
                    if j == 1 and after_b0:
                        after_b0()
                stack.walk(pe, step)

            for l in range(DEPTH):
                if l == 0:
                    pe.wait_ge(s["in_cst"], 16)
                norm(l, "norm", 2 * l)
                ht_ready(l, "norm")
                mix_wait(pe, chunk(l, 0))
                for k in range(2):
                    project(l, unit(l, "zu", k), chunk(l, 0), k)
                empty_wait(unit(l, "zu", 1))
                pe.wait_ge(s["in_b"], 16 * (l + 1))
                bu(l, 0)
                pe.wait_ge(s["cw_ready"], l + 1)
                for i in range(ST):
                    if i + 1 < ST:
                        bu(l, i + 1)
                    if i < 6:
                        zqkv(l, i)
                    for h in range(HEADS):
                        attention(l, h, i - head_start(h))
                    if i >= ST - 2:
                        u = unit(l, "oss", i - (ST - 2))
                        free(u)
                        empty_wait(unit(l, "head", 4 * (HEADS - 1) + S_OUT))
                        mm(ps[:, bank(u), :], ones, osq[:, i - (ST - 2)].rearrange("p a t -> p (a t)"), start=True,
                           stop=True).then_inc(s["unit_done"], 1)
                    if i:
                        outputs(l, i - 1)
                outputs(l, ST - 1)
                c = chunk(l, 4)
                mix_wait(pe, c)
                pe.wait_ge(s["g_ready"], FT * (l + 1))
                for k in range(2):
                    for j in range(2):
                        n = 2 * k + j
                        for f in range(FT):
                            ins = mm(ps[:, k, j * 256:j * 256 + 256], mixw[:, c % 2, f, n * P:(n + 1) * P],
                                     yq[:, f], start=(f == 0), stop=(f == FT - 1))
                    ins.then_inc(s["glu_done"], 1)

                def out_half(k, fs):
                    u = unit(l, "out", k)
                    c = chunk(l, 5 + k // 2)
                    if fs[0] and k % 2 == 0:
                        mix_wait(pe, c)
                    if fs[0]:
                        free(u)
                    t = k % 2
                    for f in fs:
                        ins = mm(ps[:, bank(u), :], cat[:, f, t * P:(t + 1) * P], mixw[:, c % 2, f, :],
                                 start=(f == FT), stop=(f == FT - 1))
                    if not fs[0]:
                        ins.then_inc(s["unit_done"], 1)

                pe.wait_ge(s["cat_ready"], 2 * l + 1)
                for k in range(4):
                    out_half(k, range(FT, KT))
                pe.wait_ge(s["qs_ready"], l + 1)
                for f in range(FT):
                    ins = mm(ps[:, 2, 0:SEQ], ones, th[:, f], start=(f == 0), stop=(f == FT - 1))
                ins.then_inc(s["gss_done"], 1)
                pe.wait_ge(s["cat_ready"], 2 * l + 2)
                for k in range(4):
                    out_half(k, range(FT))
                norm(l, "fnorm", 2 * l + 1)
                ht_ready(l, "fnorm")
                if l == 0:
                    pe.wait_ge(s["xl_done"], 1)
                    stream(Stack(None), TT)

            pe.wait_ge(s["in_wr"], 16)
            for t in range(TT):
                for f in range(KT):
                    ins = mm(ps[:, 4, t * NE:(t + 1) * NE], hT[:, f, t * P:(t + 1) * P], wr[:, f, :],
                             start=(f == 0), stop=(f == KT - 1))
            ins.then_inc(s["lg_done"], 1)
            pe.wait_ge(s["sel_ready"], 1)
            tri = cst[:, C_TRI:C_TRI + P]
            mm(ps[:, 5, 0:NE], tri, rt[:, 4, 0], start=True, stop=True)
            mm(ps[:, 5, NE:2 * NE], ones, rt[:, 4, 0], start=True, stop=False)
            mm(ps[:, 5, NE:2 * NE], tri, rt[:, 4, 1], start=False, stop=True)
            mm(ps[:, 5, 2 * NE:3 * NE], ones, rt[:, 4, 0], start=True, stop=False)
            mm(ps[:, 5, 2 * NE:3 * NE], ones, rt[:, 4, 1], start=False, stop=True).then_inc(s["pos_done"], 1)

            def gather(m, added):
                pe.wait_ge(s["picked"], m + 1)
                at_least(pe, "added", added)
                for f in range(KT):
                    for t in range(TT):
                        ins = mm(ps[:, 4 + f // 4, (f % 4) * P:(f % 4 + 1) * P], hn[:, t, f * P:(f + 1) * P],
                                 pick[:, 0, t], start=(t == 0), stop=(t == TT - 1))
                ins.then_inc(s["gathered"], 1)

            def scatter(m):
                pe.wait_ge(s["wt_ready"], m + 1)
                pe.wait_ge(s["acc_act"], m + 1)
                pe.wait_ge(s["acc_dve"], m + 1)
                for k in range(2 * TT):
                    if k == 3:
                        pe.wait_ge(s["added"], 2 * TT * m + 1)
                    t, n = k // 2, k % 2
                    mm(ps[:, SCATTER[k]], wT[:, t * P:(t + 1) * P], ybuf[:, n * 512:(n + 1) * 512],
                       start=True, stop=True).then_inc(s["scattered"], 1)

            def expert(m, prev, more):
                def middle():
                    pe.wait_ge(s["weighed"], m + 1)
                    if prev:
                        pe.wait_ge(s["added"], 2 * TT * m)
                    for t in range(TT):
                        ins = nc.tensor.transpose(ps[:, 7, t * P:(t + 1) * P], pick[:, 1, t], ident)
                    ins.then_inc(s["wt_done"], 1)
                    if more:
                        gather(m + 1, 2 * TT * m)
                pe.wait_ge(s["xl_done"], m + 2)
                stream(Stack(m), 1, (lambda: scatter(m - 1)) if prev else None, middle)

            gather(0, 0)
            expert(0, False, True)
            with pe.Fori(1, NE - 1) as e:
                expert(e, True, True)
            expert(NE - 1, True, False)
            scatter(NE - 1)
            pe.wait_ge(s["tables_ready"], 1)
            m = pe.alloc_register("pe_pass")
            pe.reg_mov(m, NE)
            with pe.Fori(0, NE) as e:
                c = pe.value_load(cnt[0:1, bass.ds(e, 1)], min_val=0, max_val=SEQ)
                with pe.If(c > CAP):
                    n = pe.snap(m, min_val=NE, max_val=2 * NE)
                    pe.wait_ge(s["added"], 2 * TT * n)
                    gather(n, 2 * TT * n)
                    expert(n, False, False)
                    scatter(n)
                    pe.reg_add(m, m, 1)


def constants():
    c = np.zeros((P, C_N), np.float32)
    p = np.arange(P)
    c[:, C_ID:C_ID + P] = np.eye(P)
    c[:, C_ONE:C_ONE + P] = 1.0
    c[:, C_TRI:C_TRI + P] = p[:, None] < p[None, :]
    for q in range(TT):
        c[:, C_DIST + q * SEQ:C_DIST + (q + 1) * SEQ] = np.abs(p[:, None] + q * P - np.arange(SEQ)[None, :])
    c[:, C_T:C_T + SEQ] = np.arange(SEQ)
    c[:, C_SLOT:C_SLOT + P] = p
    c[:, C_E8:C_E8 + 16] = np.tile(np.arange(NE) - NE, 2)
    return c


def kernel(**inputs):
    import concourse.bacc as bacc
    from concourse.bass_utils import run_bass_kernel_spmd

    a = {k: np.asarray(v) for k, v in inputs.items()}
    f32 = np.float32

    def by_feature(g, n):
        return g.reshape(DEPTH, n, P).transpose(0, 2, 1)

    def by_state(g):
        return g.reshape(DEPTH, 2, GP, 2, STATE).transpose(0, 3, 4, 2, 1).reshape(DEPTH, P, ST)

    def on_all(r):
        return np.broadcast_to(r[:, None, :], (r.shape[0], P, r.shape[1]))

    step = np.broadcast_to(a["ssm_log_step"][..., None], a["ssm_lambda_re"].shape)
    par = np.concatenate([
        by_feature(a["g_mix"], KT), by_feature(a["g_ffn"], KT), by_feature(a["ssm_d"], FT),
        by_feature(a["b_glu"], FT), by_feature(a["g_ssm_out"], FT), by_feature(a["g_subln"], 1),
        by_state(a["ssm_lambda_re"]), by_state(a["ssm_lambda_im"]), by_state(step),
        on_all(np.concatenate([a["lambda_q1"], a["lambda_k1"], a["lambda_q2"], a["lambda_k2"]], 1)),
        on_all(np.broadcast_to(a["b_router"], (DEPTH, NE)))], 2)
    rows = on_all(np.concatenate([a["g_ffn"][1], a["g_final"]])[None])[0]

    bmat = np.zeros((DEPTH, 4, 2, GROUP, FT, 2, 2, 2, STATE), f32)
    cmat = np.zeros((DEPTH, 2, STATE, 2, FT, 4, 2, 2, GROUP), f32)
    for r, (b, c) in enumerate((("ssm_b_re", "ssm_c_re"), ("ssm_b_im", "ssm_c_im"))):
        b6 = a[b].reshape(DEPTH, 2, FT, 4, 2, STATE, GROUP)
        c6 = a[c].reshape(DEPTH, 2, FT, 4, 2, GROUP, STATE)
        for g in range(2):
            bmat[:, :, g, :, :, :, r, g, :] = b6[:, :, :, :, g].transpose(0, 3, 5, 2, 1, 4)
            cmat[:, g, :, r, :, :, :, g, :] = c6[:, :, :, :, g].transpose(0, 5, 2, 3, 1, 4)
    bmat = bmat.reshape(DEPTH, P, FT, 2, 2, P)
    cmat = cmat.reshape(DEPTH, P, 2, ST, 32)

    def chunks(w, kt, n):
        return w.reshape(DEPTH, kt, P, n, 512).transpose(0, 3, 2, 1, 4)

    wmix = np.concatenate([chunks(a["w_in"], KT, 4), chunks(a["w_out"], KT, 2)], 1)
    wglu = chunks(a["w_glu"], FT, 1)[:, 0]
    wrouter = a["w_router"][0].reshape(KT, P, NE).transpose(1, 0, 2)

    def ffn(gate, up, down, nch):
        n, _, dff = gate.shape
        pad = ((0, 0), (0, 0), (0, nch * HC - dff))
        gu = np.stack([np.pad(w, pad).reshape(n, 2, 4, P, nch, HC) for w in (gate, up)])
        gu = gu.transpose(1, 5, 2, 4, 3, 0, 6).reshape(n, nch, 2, P, PIECE)
        dn = np.pad(down, ((0, 0), pad[2], (0, 0))).reshape(n, nch, 2, P, D).transpose(0, 1, 3, 2, 4)
        dn = dn.reshape(n, nch, P, PIECE)
        out = [gu[:, 0, 0], gu[:, 0, 1]]
        for c in range(1, nch):
            out += [gu[:, c, 0], gu[:, c, 1], dn[:, c - 1]]
        out.append(dn[:, nch - 1])
        return np.stack(out, 1).reshape(n * 3 * nch, P, PIECE)

    wffn = np.concatenate([
        ffn(a["dense_w_gate"], a["dense_w_up"], a["dense_w_down"], NC_D),
        ffn(a["moe_w_gate"][0], a["moe_w_up"][0], a["moe_w_down"][0], NC_E)])
    arrays = {
        "x_in": a["x"][0].reshape(TT, P, D).transpose(1, 0, 2),
        "consts": constants(), "rows": rows, "params": par.transpose(1, 0, 2), "bmat": bmat, "cmat": cmat,
        "wmix": wmix, "wglu": wglu, "wrouter": wrouter, "wffn": wffn,
    }
    arrays = {k: np.ascontiguousarray(v, dtype=f32) for k, v in arrays.items()}

    nc = bacc.Bacc("TRN2", target_bir_lowering=False, num_devices=1)
    aps = [nc.dram_tensor(k, v.shape, F32, kind="ExternalInput").ap() for k, v in arrays.items()]
    out = nc.dram_tensor("y_out", (P, TT, D), F32, kind="ExternalOutput").ap()
    encoder(nc, *aps, out)
    got = run_bass_kernel_spmd(nc, [arrays], core_ids=[0]).results[0]["y_out"]
    return np.ascontiguousarray(got.transpose(1, 0, 2)).reshape(1, SEQ, D)
```

```python
import math
from contextlib import ExitStack

import numpy as np

import concourse.bass as bass
from concourse import mybir

ALU = mybir.AluOpType
ACT = mybir.ActivationFunctionType
F32 = mybir.dt.float32
F32R = mybir.dt.float32r
I32 = mybir.dt.int32
AX = mybir.AxisListType

P = 128
D = 1024
KT = D // P
SEQ = 256
TT = SEQ // P
DEPTH = 2
SW = 512
FT = SW // P
GROUP, STATE = 16, 64
NG = SW // GROUP
GP = NG // 2
ST = GP * 2
HEADS, HD = 4, 64
DFF, DFF_E, NE = 2752, 3584, 8
HC = 2 * P
NC_D = -(-DFF // HC)
NC_E = DFF_E // HC
PIECE = 4 * 2 * HC
RING = 6
AHEAD = 4
SKIP = 3
CAP = P
EPS = 1e-6
ROUND = 1.5 * 2.0 ** 23
INV2PI = 1.0 / (2.0 * math.pi)
TWOPI = 6.283185
GELU_C = math.sqrt(2.0 / math.pi)
LINIT = [0.8 - 0.6 * math.exp(-0.3 * i) for i in range(DEPTH)]
SLOPES = [2.0 ** (-8.0 * (h + 1) / HEADS) for h in range(HEADS)]

C_ID, C_ONE, C_TRI, C_DIST, C_T, C_SLOT, C_E8 = 0, 128, 256, 384, 896, 1152, 1280
C_N = 1296
Q_GMIX, Q_GFFN, Q_D, Q_BGLU, Q_GSSM, Q_GSUB, Q_LRE, Q_LIM, Q_LS, Q_LQ, Q_BR = 0, 8, 16, 20, 24, 28, 29, 61, 93, 125, 381
Q_N = Q_BR + NE

ZQKV_AT = (0, 1, 2, 4, 6, 8)
HEAD_AT = [9 + 4 * h for h in range(HEADS)]
ATN_AT = [HEAD_AT[2 * b + 1] + 6 for b in range(HEADS // 2)]
T_EXP, T_PROBS, T_TURN, T_OUT = 2, 3, 4, 5


def beside(i):
    work = []
    for h in range(HEADS):
        at = i - HEAD_AT[h]
        if at == 0:
            work += [(f"map{h}.{m}", "D") for m in range(2)]
        elif at == T_TURN:
            work.append((f"turn{h}", "A"))
        elif at == T_OUT:
            work.append((f"head{h}", "A"))
    for b, first in enumerate(ATN_AT):
        if i == first:
            work.append((f"oms{b}", "A"))
        if first <= i < first + 4:
            n = 2 * (i - first)
            work += [(f"atn{2 * b + k // 4}.{k % 4}", "D") for k in (n, n + 1)]
    return work


UNITS = ([("norm", "D"), ("norm", "A")] * 2 + [("zu", "A")] * 2 + [("zqkv", "A")] * 6
         + [w for i in range(ST) for w in beside(i)] + [("glu", "A")] * 2 + [("out", "D")] * 4 + [("fnorm", "D"), ("fnorm", "A")] * 2)
UL = len(UNITS)
FIRST = {}
for _i, (_s, _) in enumerate(UNITS):
    FIRST.setdefault(_s, _i)
RING0, RINGN = 4, 4
SCATTER = (4, 5, 7, 4)


def unit(l, stage, k=0):
    return l * UL + FIRST[stage] + k


def emptied(u):
    who = UNITS[u % UL][1]
    return who, (u // UL) * sum(w == who for _, w in UNITS) + sum(w == who for _, w in UNITS[:u % UL + 1])


def added_here(i):
    return i <= ZQKV_AT[-1]


N_ADDED = sum(added_here(i) for i in range(ST))


def bank(u):
    return RING0 + u % RINGN


def encoder(nc, x, consts, rows, params, bmat, cmat, wmix, wglu, wrouter, wffn, out):
    with ExitStack() as ctx:
        scope = [ctx]

        def sb(name, shape, dt=F32):
            return scope[0].enter_context(nc.sbuf_tensor(name, shape, dt))

        def sem(name):
            return ctx.enter_context(nc.semaphore(name))

        ps = ctx.enter_context(nc.psum_tensor("ps", [P, 8, 512], F32))

        X = sb("X", [P, TT, D])
        hn = sb("hn", [P, TT, D])
        hT = sb("hT", [P, KT, SEQ])
        raw = sb("raw", [P, RING, PIECE])
        cst = sb("cst", [P, C_N])
        par = sb("par", [P, DEPTH, Q_N])
        wr = sb("wr", [P, KT, NE])
        rt = sb("rt", [P, 8, TT, NE])
        cnt = sb("cnt", [1, NE], I32)
        col = sb("col", [P, 96])

        scope[0] = ExitStack()
        wh = sb("wh", [P, RING, PIECE], F32R)
        wl = sb("wl", [P, RING, PIECE], F32R)
        xh = sb("xh", [P, KT, SEQ], F32R)
        xl = sb("xl", [P, KT, SEQ], F32R)
        hidh = sb("hidh", [P, 2, SEQ], F32R)
        hidl = sb("hidl", [P, 2, SEQ], F32R)
        hv = sb("hv", [P, 2, HC])
        pick = sb("pick", [P, 2, TT, CAP])
        wT = sb("wT", [P, SEQ])
        ybuf = sb("ybuf", [P, D])
        scope[0].close()

        scope[0] = ctx
        mixw = sb("mixw", [P, 2, KT, 512])
        bw = sb("bw", [P, FT, 2, 2, P])
        small = sb("small", [P, 16, ST])
        cw = sb("cw", [P, 2, ST, 32])
        work = sb("work", [P, 33 * SEQ])

        def part(at, *shape):
            names = "abcd"[:len(shape)]
            sizes = dict(zip(names, shape))
            flat = work[:, at * SEQ:at * SEQ + math.prod(shape) * SEQ]
            return flat.rearrange(f"p ({' '.join(names)} t) -> p {' '.join(names)} t", **sizes)

        phase = part(0, 2)
        turns = part(2, 2, 2)
        trig = part(6, 3, 3)
        ri1 = part(15, 2)
        ri2 = part(17, 2)
        st = part(19, 3, 2)
        ro = part(25, 2, 2, 2)
        S = hn[:, 0].rearrange("p (m q t) -> p m q t", m=2, q=TT)
        A = hn[:, 1].rearrange("p (h q t) -> p h q t", h=2, q=TT)
        AT = hT[:, 0:4].rearrange("p (h k) t -> p h k t", h=2)
        osq = hT[:, 4:8].rearrange("p (k a) t -> p k a t", k=2)
        uT = sb("uT", [P, FT, SEQ])
        qk = sb("qk", [P, 2, HEADS, SEQ])
        qT, kT = qk[:, 0], qk[:, 1]
        wg = qk[:].rearrange("p a (f b) t -> p (a f) (b t)", b=2)
        v = sb("v", [P, TT, 512])
        cat = sb("cat", [P, KT, SEQ])
        yt = sb("yt", [P, FT, SEQ])
        yq = sb("yq", [P, FT, SEQ])
        th = sb("th", [P, FT, SEQ])
        craw = cat[:].rearrange("p (r a) (b n) -> p r (a b) n", r=2, n=32)
        ctmp = yt[:].rearrange("p a (b n) -> p (a b) n", n=32)

        ident = cst[:, C_ID:C_ID + P]
        ones = cst[:, C_ONE:C_ONE + P]

        names = """in_x in_cst in_par in_b in_c in_glu in_wr out_done unit_done emptied_act emptied_dve act_chain
            dve_chain sumsq rstd hn_ready small_act small_dve cw_ready phase_ready frac_ready trig_ready bu_ready
            bu_read ri_ready scanned summed c_done y_read gin gtanh g_ready gss_done gss_root qs_ready
            score_ready exp_done att_ready cat_ready hi_done lo_done piece_done xh_done xl_done silu_done
            hv_ready turned hid_hi hid_lo dense_added lg_done routed_exp ex_done picked weighed gathered wt_done
            wt_ready acc_act acc_dve scattered added mixer_done gain_in sel_ready pos_done tables_ready xh_ready
            final_ready products""".split()
        s = {n: sem(n) for n in names}
        mix_full = [sem(f"mix_full{i}") for i in range(2)]
        raw_full = [sem(f"raw_full{i}") for i in range(RING)]

        block = ctx.enter_context(nc.Block())

        def chunk(l, k):
            return 6 * l + k

        def last_use(c):
            stage, k = [("zu", 1), ("zqkv", 1), ("zqkv", 3), ("zqkv", 5)][c % 6]
            return unit(c // 6, stage, k)

        def mix_wait(eng, c):
            eng.wait_ge(mix_full[c % 2], 16 * (c // 2 + 1))

        class Stack:

            def __init__(self, m):
                self.moe, self.n = m is not None, NC_D if m is None else NC_E
                self.shift = 0 if self.moe else SKIP
                self.m = 0 if m is None else m
                self.q0, self.c0, self.k0 = (3 * NC_D, NC_D, (3 * NC_D + SKIP) // RING) if self.moe else (0, 0, 0)

            def slot(self, j):
                return (j + self.shift) % RING

            def piece(self, j, g):
                return self.m * (3 * NC_E) + g * RING + (self.q0 + j)

            def chunk(self, c, g):
                return self.m * NC_E + g * 2 + (self.c0 + c)

            def loads(self, j, g):
                turns = self.m * (3 * NC_E // RING) + g + (self.k0 + (j + self.shift) // RING)
                return turns * 16 + (0 if self.slot(j) < SKIP else 16)

            def walk(self, eng, step):
                order = [("A", 0), ("B", 0)]
                for c in range(1, self.n):
                    order += [("A", c), ("B", c), ("D", c - 1)]
                order.append(("D", self.n - 1))
                turns = (self.n - 1) // 2
                for j in range(8):
                    step(j, 0, *order[j])
                peeled = 0 if self.moe else 1
                with eng.Fori(1, turns - peeled) as g:
                    for j in range(2, 8):
                        step(j, g, *order[j])
                for j in range(2, 8) if peeled else ():
                    step(j, turns - 1, *order[j])
                for j in range(2 + 6 * turns, 3 * self.n):
                    step(j, 0, *order[j])

        def at_least(eng, what, n):
            if not isinstance(n, int) or n > 0:
                eng.wait_ge(s[what], n)

        @block.sync
        def _(sp):
            sp.dma_start(X[:], x).then_inc(s["in_x"], 16)
            sp.dma_start(par[:], params).then_inc(s["in_par"], 16)
            sp.dma_start(cst[:], consts).then_inc(s["in_cst"], 16)

            def mix(l, k):
                c = chunk(l, k)
                if k >= 2:
                    sp.wait_ge(s["unit_done"], last_use(c - 2) + 1)
                sp.dma_start(mixw[:, c % 2], wmix[l, k]).then_inc(mix_full[c % 2], 16)

            def glu(l):
                sp.wait_ge(s["unit_done"], unit(l, f"map{HEADS - 1}.1") + 1)
                sp.dma_start(wg, wglu[l]).then_inc(s["in_glu"], 16)

            def load(slot, index, free):
                if free is not None:
                    sp.wait_ge(s["lo_done"], free)
                src = wffn[index] if isinstance(index, int) else wffn[bass.ds(index, 1)].rearrange("a p n -> p (a n)")
                sp.dma_start(raw[:, slot], src).then_inc(raw_full[slot], 16)

            mix(0, 0)
            mix(0, 1)
            sp.dma_start(wr[:], wrouter).then_inc(s["in_wr"], 16)
            for q in range(RING):
                load((q + SKIP) % RING, q, None)
            for k in range(2, 6):
                mix(0, k)
            glu(0)
            with sp.Fori(1, 3 * NC_D // RING) as g:
                for j in range(RING):
                    load((j + SKIP) % RING, RING * g + j, RING * g + (j - RING + 1))
            for q in range(3 * NC_D // RING * RING, 3 * NC_D):
                load((q + SKIP) % RING, q, q - RING + 1)
            base = 3 * NC_D
            for j in range(RING):
                load(j, base + j, base + j - RING + 1)
            sp.wait_ge(s["piece_done"], base)
            for k in range(6):
                mix(1, k)
            glu(1)
            with sp.Fori(1, NE * 3 * NC_E // RING) as g:
                for j in range(RING):
                    load(j, RING * g + (base + j), RING * g + (base + j - RING + 1))
            sp.wait_ge(s["tables_ready"], 1)
            m = sp.alloc_register("sp_pass")
            sp.reg_mov(m, NE)
            with sp.Fori(0, NE) as e:
                c = sp.value_load(cnt[0:1, bass.ds(e, 1)], min_val=0, max_val=SEQ)
                with sp.If(c > CAP):
                    n = sp.snap(m, min_val=NE, max_val=2 * NE)
                    with sp.Fori(0, 3 * NC_E // RING) as g:
                        for j in range(RING):
                            load(j, 3 * NC_E * e + RING * g + (base + j),
                                 3 * NC_E * n + RING * g + (base + j - RING + 1))
                    sp.reg_add(m, m, 1)
            for t in range(TT):
                sp.wait_ge(s["final_ready"], t + 1)
                sp.dma_start(out[:, t], hn[:, t]).then_inc(s["out_done"], 16)
            sp.wait_ge(s["out_done"], 16 * TT)

        @block.gpsimd
        def _(pool):
            for l in range(DEPTH):
                if l:
                    pool.wait_ge(s["piece_done"], 3 * NC_D)
                pool.dma_start(bw[:], bmat[l]).then_inc(s["in_b"], 16)
                pool.dma_start(craw[:], cmat[l]).then_inc(s["in_c"], 16)
                for i in range(ST):
                    n = ST * l + i
                    b = i % 2
                    pool.wait_ge(s["scanned"], n + 1)
                    if n >= 2:
                        pool.wait_ge(s["c_done"], n - 1)
                    nc.gpsimd.tensor_tensor(ro[:, b, 0], st[:, n % 3], trig[:, n % 3, 0:1, :].to_broadcast([P, 2, SEQ]),
                                            ALU.mult)
                    nc.gpsimd.tensor_tensor(ro[:, b, 1], st[:, n % 3, ::-1, :], trig[:, n % 3, 2:0:-1, :],
                                            ALU.mult).then_inc(s["products"], 1)
                    if added_here(i):
                        pool.wait_ge(s["products"], n + 1)
                        nc.gpsimd.tensor_tensor(ro[:, b, 0], ro[:, b, 0], ro[:, b, 1],
                                                ALU.add).then_inc(s["summed"], 1)
            pool.wait_ge(s["mixer_done"], 1)
            pool.dma_start(ybuf[:], rows[:, 0:D]).then_inc(s["gain_in"], 16)
            pool.wait_ge(s["xh_ready"], 1)
            pool.dma_start(ybuf[:], rows[:, D:2 * D]).then_inc(s["gain_in"], 16)

        @block.scalar
        def _(act):
            chain = [0]

            def link(ins):
                chain[0] += 1
                ins.then_inc(s["act_chain"], 1)
                act.wait_ge(s["act_chain"], chain[0])

            def full(u):
                act.wait_ge(s["unit_done"], u + 1)

            def norm_squares(m, tokens_ready=None):
                for t in range(TT):
                    if tokens_ready:
                        tokens_ready(t)
                    ins = nc.scalar.activation(hn[:, t], X[:, t], ACT.Square, accum_out=col[:, 2 * t:2 * t + 1])
                ins.then_inc(s["sumsq"], 1)
                act.wait_ge(s["rstd"], 2 * m + 1)
                nc.scalar.activation(col[:, 8:10], col[:, 4:6], ACT.Sqrt).then_inc(s["small_act"], 1)

            def norm_empty(l, stage, gain):
                for k in (1, 3):
                    full(unit(l, stage, k))
                    for j in range(2):
                        f = 2 * k + j
                        ins = nc.scalar.activation(hT[:, f, :], ps[:, bank(unit(l, stage, k)), j * 256:j * 256 + 256],
                                                   ACT.Copy, scale=par[:, l, gain + f:gain + f + 1])
                    ins.then_inc(s["emptied_act"], 1)

            def phases(l, i):
                n = ST * l + i
                act.wait_ge(s["small_dve"], 4 * l + 4)
                if n:
                    act.wait_ge(s["frac_ready"], n)
                nc.scalar.activation(phase[:, 0], cst[:, C_T:C_T + SEQ], ACT.Copy, scale=small[:, 4, i:i + 1])
                chain[0] += 1
                nc.scalar.activation(phase[:, 1], cst[:, C_T:C_T + SEQ], ACT.Identity, bias=col[:, 17:18],
                                     scale=small[:, 4, i:i + 1]).then_inc(s["act_chain"], 1)

            def nearest(l, i):
                act.wait_ge(s["act_chain"], chain[0])
                if ST * l + i >= 2:
                    act.wait_ge(s["trig_ready"], ST * l + i - 1)
                nc.scalar.activation(turns[:, i % 2], phase[:], ACT.Copy, bias=ROUND).then_inc(s["phase_ready"], 1)

            def trigs(l, i, between=None):
                n = ST * l + i
                act.wait_ge(s["frac_ready"], n + 1)
                if n >= 3:
                    act.wait_ge(s["products"], n - 2)
                nc.scalar.activation(trig[:, n % 3, 0], turns[:, i % 2, 1], ACT.Sin, scale=-TWOPI)
                if between:
                    between()
                nc.scalar.activation(trig[:, n % 3, 1], turns[:, i % 2, 0], ACT.Sin, scale=-TWOPI)
                nc.scalar.activation(trig[:, n % 3, 2], turns[:, i % 2, 0], ACT.Sin,
                                     scale=TWOPI).then_inc(s["trig_ready"], 1)

            def gelu_tanh(l, ft):
                act.wait_ge(s["gin"], FT * l + ft + 1)
                nc.scalar.activation(th[:, ft], th[:, ft], ACT.Tanh, scale=GELU_C).then_inc(s["gtanh"], 1)

            def attention(l, h, at):
                if at == T_EXP:
                    for m in range(2):
                        act.wait_ge(s["score_ready"], 2 * (HEADS * l + h) + m + 1)
                        for q in range(TT):
                            c = 4 * (h % 2) + 2 * m + q
                            ins = nc.scalar.activation(S[:, m, q], S[:, m, q], ACT.Exp, bias=col[:, 64 + c:65 + c],
                                                       accum_out=col[:, 72 + c:73 + c])
                    ins.then_inc(s["exp_done"], 1)
                elif at == T_TURN:
                    u = unit(l, f"turn{h}")
                    full(u)
                    nc.scalar.activation(AT[:, h % 2], ps[:, bank(u)].rearrange("p (k t) -> p k t", k=TT),
                                         ACT.Copy).then_inc(s["emptied_act"], 1)
                elif at == T_OUT:
                    u = unit(l, f"head{h}")
                    full(u)
                    nc.scalar.activation(cat[:, FT + h], ps[:, bank(u), 0:SEQ], ACT.Copy, scale=col[:, 15:16])
                    nc.scalar.activation(osq[:, h // 2, h % 2], ps[:, bank(u), 0:SEQ],
                                         ACT.Square).then_inc(s["emptied_act"], 1)

            def upper(stack, j, g):
                q, slot = stack.piece(j, g), stack.slot(j)
                act.wait_ge(raw_full[slot], stack.loads(j, g))
                at_least(act, "piece_done", q - (RING - 1))
                nc.scalar.activation(wh[:, slot], raw[:, slot], ACT.Copy).then_inc(s["hi_done"], 1)

            def stream(stack, nt, more, middle=None):
                w = nt * P

                def hidden_upper(c, g):
                    act.wait_ge(s["turned"], stack.chunk(c, g) + 1)
                    nc.scalar.activation(hidh[:, :, 0:w], ps[:, 6, 0:2 * w].rearrange("p (a t) -> p a t", a=2),
                                         ACT.Copy).then_inc(s["hid_hi"], 1)

                def step(j, g, kind, c):
                    if more or not isinstance(g, int) or j + RING * g + AHEAD < 3 * stack.n:
                        upper(stack, j + AHEAD, g)
                    if kind == "A" and c:
                        hidden_upper(c - 1, g)
                    if kind == "B":
                        k = stack.chunk(c, g)
                        act.wait_ge(s["piece_done"], stack.piece(j, g) + 1)
                        at_least(act, "turned", k)
                        b = c % 2 if nt == 1 else 0
                        nc.scalar.activation(hv[:, 0:nt], ps[:, b:b + nt, 0:HC], ACT.Silu).then_inc(s["silu_done"], 1)
                    if j == 3 * stack.n - 1:
                        hidden_upper(c, g)
                        if middle:
                            middle()
                stack.walk(act, step)

            for l in range(DEPTH):
                if l == 0:
                    act.wait_ge(s["in_par"], 16)
                    act.wait_ge(s["in_x"], 16)
                else:
                    act.wait_ge(s["dense_added"], 1)
                norm_squares(2 * l)
                norm_empty(l, "norm", Q_GMIX)
                pr = par[:, l]
                nc.scalar.activation(small[:, 0], pr[:, Q_LS:Q_LS + ST], ACT.Exp).then_inc(s["small_act"], 1)
                act.wait_ge(s["small_dve"], 4 * l + 1)
                nc.scalar.activation(small[:, 3], small[:, 1], ACT.Exp)
                nc.scalar.activation(col[:, 12:14], col[:, 10:12], ACT.Exp).then_inc(s["small_act"], 1)
                act.wait_ge(s["small_dve"], 4 * l + 2)
                nc.scalar.activation(small[:, 5:7], small[:, 7:9], ACT.Sin, scale=-TWOPI).then_inc(s["small_act"], 1)

                phases(l, 0)
                nearest(l, 0)
                for k in range(2):
                    u = unit(l, "zu", k)
                    full(u)
                    nc.scalar.activation(uT[:, 2 * k:2 * k + 2, :], ps[:, bank(u)].rearrange("p (a t) -> p a t", a=2),
                                         ACT.Copy).then_inc(s["emptied_act"], 1)
                phases(l, 1)
                trigs(l, 0, lambda: nearest(l, 1))
                for i in range(ST):
                    if i + 2 < ST:
                        phases(l, i + 2)
                        trigs(l, i + 1, lambda: nearest(l, i + 2))
                    elif i + 1 < ST:
                        trigs(l, i + 1)
                    if i - 1 in ZQKV_AT:
                        k = ZQKV_AT.index(i - 1)
                        u = unit(l, "zqkv", k)
                        full(u)
                        pb = ps[:, bank(u)]
                        if k < 4:
                            dst = (qT, kT)[k // 2][:, 2 * (k % 2):2 * (k % 2) + 2, :]
                            nc.scalar.activation(dst, pb.rearrange("p (a t) -> p a t", a=2), ACT.Copy,
                                                 scale=(HD ** -0.5 if k < 2 else 1.0)).then_inc(s["emptied_act"], 1)
                        else:
                            nc.scalar.activation(v[:, k - 4], pb, ACT.Copy).then_inc(s["emptied_act"], 1)
                    for h in range(HEADS):
                        attention(l, h, i - HEAD_AT[h])
                    if i - 1 in ATN_AT:
                        b = ATN_AT.index(i - 1)
                        u = unit(l, f"oms{b}")
                        full(u)
                        nc.scalar.activation(col[:, 24 + 4 * b:28 + 4 * b], ps[:, bank(u), 0:2 * TT], ACT.Sqrt,
                                             bias=col[:, 18:19], scale=1.0 / (2 * HD)).then_inc(s["emptied_act"], 1)
                    if i % 8 == 1 and i > 1:
                        gelu_tanh(l, i // 8 - 1)
                gelu_tanh(l, FT - 1)
                for k in range(2):
                    u = unit(l, "glu", k)
                    full(u)
                    for j in range(2):
                        f = 2 * k + j
                        ins = nc.scalar.activation(th[:, f], ps[:, bank(u), j * 256:j * 256 + 256], ACT.Tanh,
                                                   bias=col[:, 20 + f:21 + f], scale=0.25)
                    ins.then_inc(s["emptied_act"], 1)
                act.wait_ge(s["gss_done"], l + 1)
                nc.scalar.activation(col[:, 32:34], ps[:, 2, 0:TT], ACT.Sqrt, bias=col[:, 19:20],
                                     scale=1.0 / SW).then_inc(s["gss_root"], 1)

                stack = Stack(None if l == 0 else 0)
                norm_squares(2 * l + 1, lambda t: act.wait_ge(s["emptied_dve"], emptied(unit(l, "out", 2 * t + 1))[1]))
                upper(stack, 0, 0)
                upper(stack, 1, 0)
                norm_empty(l, "fnorm", Q_GFFN)
                if l == 0:
                    act.wait_ge(s["emptied_dve"], emptied(unit(l, "fnorm", 2))[1])
                    act.wait_ge(s["emptied_act"], emptied(unit(l, "fnorm", 3))[1])
                    nc.scalar.activation(xh[:], hT[:], ACT.Copy).then_inc(s["xh_done"], 1)
                for j in range(2, AHEAD):
                    upper(stack, j, 0)
                if l == 0:
                    stream(stack, TT, False)

            act.wait_ge(s["routed_exp"], 1)
            nc.scalar.activation(col[:, 44:46], col[:, 40:42], ACT.Exp).then_inc(s["ex_done"], 1)

            def gather(m):
                act.wait_ge(s["gathered"], m + 1)
                nc.scalar.activation(xh[:, :, 0:CAP], ps[:, 4:6].rearrange("p b (a t) -> p (b a) t", a=4),
                                     ACT.Copy).then_inc(s["xh_done"], 1)

            def expert(m, more):
                stack = Stack(m)

                def middle():
                    act.wait_ge(s["wt_done"], m + 1)
                    nc.scalar.activation(wT[:], ps[:, 7, 0:SEQ], ACT.Copy).then_inc(s["wt_ready"], 1)
                    if more:
                        gather(m + 1)
                stream(stack, 1, more, middle)
                act.wait_ge(s["piece_done"], stack.piece(3 * NC_E, 0))
                nc.scalar.activation(ybuf[:, 0:512], ps[:, 2], ACT.Copy).then_inc(s["acc_act"], 1)

            gather(0)
            expert(0, True)
            with act.Fori(1, NE - 1) as e:
                expert(e, True)
            expert(NE - 1, False)
            act.wait_ge(s["tables_ready"], 1)
            m = act.alloc_register("act_pass")
            act.reg_mov(m, NE)
            with act.Fori(0, NE) as e:
                c = act.value_load(cnt[0:1, bass.ds(e, 1)], min_val=0, max_val=SEQ)
                with act.If(c > CAP):
                    n = act.snap(m, min_val=NE, max_val=2 * NE)
                    for j in range(AHEAD):
                        upper(Stack(n), j, 0)
                    gather(n)
                    expert(n, False)
                    act.reg_add(m, m, 1)
            act.wait_ge(s["xh_ready"], 1)
            norm_squares(2 * DEPTH)

        @block.vector
        def _(dve):
            chain = [0]

            def link(ins):
                chain[0] += 1
                ins.then_inc(s["dve_chain"], 1)
                dve.wait_ge(s["dve_chain"], chain[0])

            def full(u):
                dve.wait_ge(s["unit_done"], u + 1)

            ts, tt, stt = nc.vector.tensor_scalar, nc.vector.tensor_tensor, nc.vector.scalar_tensor_tensor

            link(nc.vector.memset(col[:, 17:18], 0.25))
            link(nc.vector.memset(col[:, 18:19], EPS))
            link(nc.vector.memset(col[:, 19:20], 16 * EPS))

            small_acts = [0]

            def small_act():
                small_acts[0] += 1
                dve.wait_ge(s["small_act"], small_acts[0])

            def norm_scale(m, done="hn_ready", gain=None):
                dve.wait_ge(s["sumsq"], m + 1)
                ts(col[:, 4:6], col[:, 0:4:2], 1.0 / D, EPS, ALU.mult, ALU.add).then_inc(s["rstd"], 2)
                small_act()
                link(nc.vector.reciprocal(col[:, 6:8], col[:, 8:10]))
                if gain is not None:
                    dve.wait_ge(s["gain_in"], 32)
                for t in range(TT):
                    if gain is None:
                        ins = ts(hn[:, t], X[:, t], col[:, 6 + t:7 + t], None, ALU.mult)
                    else:
                        ins = stt(hn[:, t], X[:, t], col[:, 6 + t:7 + t], gain[:], ALU.mult, ALU.mult)
                    if t == TT - 1 or gain is not None:
                        ins.then_inc(s[done], 1)

            def norm_empty(l, stage, gain):
                for k in (0, 2):
                    u = unit(l, stage, k)
                    full(u)
                    for j in range(2):
                        f = 2 * k + j
                        ins = ts(hT[:, f, :], ps[:, bank(u), j * 256:j * 256 + 256],
                                 par[:, l, gain + f:gain + f + 1], None, ALU.mult)
                    ins.then_inc(s["emptied_dve"], 1)

            def wrap(dst, src, tmp):
                link(ts(tmp, src, ROUND, None, ALU.add))
                link(stt(dst, tmp, ROUND, src, ALU.subtract, ALU.subtract))

            def scalars(l):
                pr = par[:, l]
                sm = small
                small_act()
                link(tt(sm[:, 1], pr[:, Q_LRE:Q_LRE + ST], sm[:, 0], ALU.mult))
                link(tt(th[:, 0, 0:2 * HD].rearrange("p (a d) -> p a d", a=2),
                        pr[:, Q_LQ:Q_LQ + 4 * HD].rearrange("p (a b d) -> p a b d", a=2, b=2)[:, :, 0],
                        pr[:, Q_LQ:Q_LQ + 4 * HD].rearrange("p (a b d) -> p a b d", a=2, b=2)[:, :, 1], ALU.mult))
                nc.vector.reduce_sum(col[:, 10:12], th[:, 0, 0:2 * HD].rearrange("p (a d) -> p a d", a=2),
                                     axis=AX.X).then_inc(s["small_dve"], 1)
                link(tt(sm[:, 2], pr[:, Q_LIM:Q_LIM + ST], sm[:, 0], ALU.mult))
                link(ts(sm[:, 2], sm[:, 2], INV2PI, None, ALU.mult))
                wrap(sm[:, 7], sm[:, 2], sm[:, 9])
                link(ts(sm[:, 4], sm[:, 7], -1.0, None, ALU.mult))
                link(ts(sm[:, 10], sm[:, 4], 0.25, None, ALU.add))
                link(ts(sm[:, 9], sm[:, 10], ROUND, None, ALU.add))
                stt(sm[:, 8], sm[:, 9], ROUND, sm[:, 10], ALU.subtract, ALU.subtract).then_inc(s["small_dve"], 1)
                small_act()
                link(ts(col[:, 14:15], col[:, 13:14], col[:, 12:13], -LINIT[l], ALU.subtract, ALU.add))
                link(ts(col[:, 15:16], pr[:, Q_GSUB:Q_GSUB + 1], 1.0 - LINIT[l], None, ALU.mult))
                link(ts(col[:, 20:24], pr[:, Q_BGLU:Q_BGLU + 4], 0.5, None, ALU.mult))
                small_act()
                lre, lim = pr[:, Q_LRE:Q_LRE + ST], pr[:, Q_LIM:Q_LIM + ST]
                link(tt(sm[:, 9], sm[:, 3], sm[:, 6], ALU.mult))
                link(ts(sm[:, 9], sm[:, 9], -1.0, None, ALU.add))
                link(tt(sm[:, 10], sm[:, 3], sm[:, 5], ALU.mult))
                link(tt(sm[:, 11], lre, lre, ALU.mult))
                link(tt(sm[:, 12], lim, lim, ALU.mult))
                link(tt(sm[:, 11], sm[:, 11], sm[:, 12], ALU.add))
                link(nc.vector.reciprocal(sm[:, 11], sm[:, 11]))
                link(tt(sm[:, 12], sm[:, 9], lre, ALU.mult))
                link(tt(sm[:, 13], sm[:, 10], lim, ALU.mult))
                link(tt(sm[:, 12], sm[:, 12], sm[:, 13], ALU.add))
                link(tt(sm[:, 14], sm[:, 12], sm[:, 11], ALU.mult))
                link(tt(sm[:, 12], sm[:, 10], lre, ALU.mult))
                link(tt(sm[:, 13], sm[:, 9], lim, ALU.mult))
                link(tt(sm[:, 12], sm[:, 12], sm[:, 13], ALU.subtract))
                link(tt(sm[:, 15], sm[:, 12], sm[:, 11], ALU.mult))
                ts(sm[:, 0], sm[:, 15], -1.0, None, ALU.mult).then_inc(s["small_dve"], 2)

            def fold_c(l):
                sm = small

                def b(r):
                    return sm[:, r, :].rearrange("p (t a) -> p t a", a=1).to_broadcast([P, ST, 32])
                dve.wait_ge(s["small_dve"], 4 * l + 4)
                dve.wait_ge(s["in_c"], 16 * (l + 1))
                link(tt(cw[:, 0], craw[:, 0], b(14), ALU.mult))
                link(tt(ctmp[:], craw[:, 1], b(15), ALU.mult))
                link(tt(cw[:, 0], cw[:, 0], ctmp[:], ALU.subtract))
                link(tt(cw[:, 1], craw[:, 0], b(0), ALU.mult))
                link(tt(ctmp[:], craw[:, 1], b(14), ALU.mult))
                tt(cw[:, 1], cw[:, 1], ctmp[:], ALU.subtract).then_inc(s["cw_ready"], 1)

            def fracs(l, i):
                n = ST * l + i
                dve.wait_ge(s["phase_ready"], n + 1)
                stt(turns[:, i % 2], turns[:, i % 2], ROUND, phase[:], ALU.subtract,
                    ALU.subtract).then_inc(s["frac_ready"], 1)

            def gelu_in(l, ft):
                dve.wait_ge(s["c_done"], ST * l + 8 * (ft + 1))
                y = yt[:, ft]
                stt(y, uT[:, ft], par[:, l, Q_D + ft:Q_D + ft + 1], ps[:, 2 + ft % 2, 0:SEQ],
                    ALU.mult, ALU.add).then_inc(s["y_read"], 1)
                dve.wait_ge(s["y_read"], FT * l + ft + 1)
                link(tt(th[:, ft], y, y, ALU.mult))
                link(ts(th[:, ft], th[:, ft], 0.044715, 1.0, ALU.mult, ALU.add))
                tt(th[:, ft], th[:, ft], y, ALU.mult).then_inc(s["gin"], 1)

            def gelu_out(l, ft):
                dve.wait_ge(s["gtanh"], FT * l + ft + 1)
                stt(yq[:, ft], th[:, ft], 1.0, yt[:, ft], ALU.add, ALU.mult).then_inc(s["g_ready"], 1)

            def rotate_in(l, i):
                n = ST * l + i
                b = i % 2
                dve.wait_ge(s["trig_ready"], n + 1)
                dve.wait_ge(s["bu_ready"], n + 1)
                if n:
                    dve.wait_ge(s["scanned"], n)
                bu = ps[:, b].rearrange("p (r t) -> p r t", r=2)
                tt(ri1[:], bu, trig[:, n % 3, 0:1, :].to_broadcast([P, 2, SEQ]), ALU.mult)
                tt(ri2[:], bu[:, ::-1, :], trig[:, n % 3, 1:3, :], ALU.mult).then_inc(s["bu_read"], 1)

            def add_in(l, i):
                dve.wait_ge(s["bu_read"], ST * l + i + 1)
                tt(ri1[:], ri1[:], ri2[:], ALU.add).then_inc(s["ri_ready"], 1)

            def scan(l, i):
                n = ST * l + i
                dve.wait_ge(s["ri_ready"], n + 1)
                if n >= 3:
                    dve.wait_ge(s["products"], n - 2)
                decay = small[:, 3, i:i + 1].to_broadcast([P, SEQ])
                for r in range(2):
                    ins = nc.vector.tensor_tensor_scan(st[:, n % 3, r], decay, ri1[:, r], 0.0, ALU.mult, ALU.add)
                ins.then_inc(s["scanned"], 1)

            def score(l, h, m):
                u = unit(l, f"map{h}.{m}")
                full(u)
                if HEADS * l + h:
                    dve.wait_ge(s["att_ready"], HEADS * l + h)
                dist = cst[:, C_DIST:C_DIST + TT * SEQ].rearrange("p (a t) -> p a t", a=TT)
                stt(S[:, m], dist, -SLOPES[h], ps[:, bank(u)].rearrange("p (a t) -> p a t", a=TT),
                    ALU.mult, ALU.add).then_inc(s["emptied_dve"], 1)
                dve.wait_ge(s["emptied_dve"], emptied(u)[1])
                c = 64 + 4 * (h % 2) + 2 * m
                link(nc.vector.reduce_max(col[:, 34:36], S[:, m], axis=AX.X))
                ts(col[:, c:c + 2], col[:, 34:36], -1.0, None, ALU.mult).then_inc(s["score_ready"], 1)

            def attend(l, h):
                b = h % 2
                dve.wait_ge(s["exp_done"], HEADS * l + h + 1)
                if h >= 2:
                    dve.wait_ge(s["unit_done"], unit(l, f"turn{h - 2}") + 1)
                link(nc.vector.reciprocal(col[:, 80:84], col[:, 72 + 4 * b:76 + 4 * b]))
                link(ts(col[:, 82:84], col[:, 82:84], col[:, 14:15], None, ALU.mult))
                for q in range(TT):
                    ins = ts(A[:, b, q], S[:, 1, q], col[:, 82 + q:83 + q], None, ALU.mult)
                link(ins)
                for q in range(TT):
                    ins = stt(A[:, b, q], S[:, 0, q], col[:, 80 + q:81 + q], A[:, b, q], ALU.mult, ALU.add)
                ins.then_inc(s["att_ready"], 1)

            def attention_out(l, b, at):
                if at == 0:
                    dve.wait_ge(s["emptied_act"], emptied(unit(l, f"oms{b}"))[1])
                    link(nc.vector.reciprocal(col[:, 84 + 4 * b:88 + 4 * b], col[:, 24 + 4 * b:28 + 4 * b]))
                for n in (2 * at, 2 * at + 1):
                    h, k = 2 * b + n // 4, n % 4
                    u = unit(l, f"atn{h}.{k}")
                    full(u)
                    if h:
                        dve.wait_ge(s["emptied_dve"], emptied(unit(l, f"atn{h - 1}.{k}"))[1])
                    t = k // 2
                    c = 84 + TT * h + t
                    xs = X[:, t, (k % 2) * 512:(k % 2) * 512 + 512]
                    stt(xs, ps[:, bank(u)], col[:, c:c + 1], xs, ALU.mult, ALU.add).then_inc(s["emptied_dve"], 1)

            def lower(stack, j, g):
                dve.wait_ge(s["hi_done"], stack.piece(j, g) + 1)
                slot = stack.slot(j)
                tt(wl[:, slot], raw[:, slot], wh[:, slot].bitcast(F32), ALU.subtract).then_inc(s["lo_done"], 1)

            def stream(stack, nt, more, early=None, middle=None):
                w = nt * P

                def hidden_lower(c, g):
                    dve.wait_ge(s["hid_hi"], stack.chunk(c, g) + 1)
                    tt(hidl[:, :, 0:w], ps[:, 6, 0:2 * w].rearrange("p (a t) -> p a t", a=2),
                       hidh[:, :, 0:w].bitcast(F32), ALU.subtract).then_inc(s["hid_lo"], 1)

                def step(j, g, kind, c):
                    if more or not isinstance(g, int) or j + RING * g + AHEAD < 3 * stack.n:
                        lower(stack, j + AHEAD, g)
                    if kind == "A" and c:
                        hidden_lower(c - 1, g)
                    if kind == "B":
                        k = stack.chunk(c, g)
                        dve.wait_ge(s["silu_done"], k + 1)
                        b = c % 2 if nt == 1 else 0
                        tt(hv[:, 0:nt], hv[:, 0:nt], ps[:, b:b + nt, HC:2 * HC], ALU.mult).then_inc(s["hv_ready"], 1)
                    if j == 1 and early:
                        early()
                    if j == 3 * stack.n - 1:
                        hidden_lower(c, g)
                        if middle:
                            middle()
                stack.walk(dve, step)

            for l in range(DEPTH):
                if l == 0:
                    dve.wait_ge(s["in_par"], 16)
                    dve.wait_ge(s["in_x"], 16)
                norm_scale(2 * l)
                norm_empty(l, "norm", Q_GMIX)
                scalars(l)
                fold_c(l)
                fracs(l, 0)
                fracs(l, 1)
                for i in range(ST):
                    rotate_in(l, i)
                    add_in(l, i)
                    if i + 2 < ST:
                        fracs(l, i + 2)
                    for h in range(HEADS):
                        if i == HEAD_AT[h] + 1:
                            score(l, h, 0)
                            score(l, h, 1)
                        if i == HEAD_AT[h] + T_PROBS:
                            attend(l, h)
                    for b, first in enumerate(ATN_AT):
                        if first < i <= first + 4:
                            attention_out(l, b, i - first - 1)
                    if i % 8 == 1 and i > 1:
                        gelu_in(l, i // 8 - 1)
                    if i % 8 == 2 and i > 2:
                        gelu_out(l, i // 8 - 1)
                    scan(l, i)
                gelu_in(l, FT - 1)
                gelu_out(l, FT - 1)
                for k in range(2):
                    dve.wait_ge(s["emptied_act"], emptied(unit(l, "glu", k))[1])
                    f = slice(2 * k, 2 * k + 2)
                    link(stt(yt[:, f], th[:, f], 1.0, yq[:, f], ALU.add, ALU.mult))
                    for f in range(2 * k, 2 * k + 2):
                        ins = ts(cat[:, f], yt[:, f], par[:, l, Q_GSSM + f:Q_GSSM + f + 1], None, ALU.mult)
                    ins.then_inc(s["cat_ready"], 1)
                    f = slice(2 * k, 2 * k + 2)
                    ins = tt(th[:, f], yt[:, f], yt[:, f], ALU.mult)
                ins.then_inc(s["qs_ready"], 1)
                dve.wait_ge(s["gss_root"], l + 1)
                link(nc.vector.reciprocal(col[:, 92:94], col[:, 32:34]))
                for k in range(4):
                    u = unit(l, "out", k)
                    full(u)
                    t = k // 2
                    xs = X[:, t, (k % 2) * 512:(k % 2) * 512 + 512]
                    stt(xs, ps[:, bank(u)], col[:, 92 + t:93 + t], xs, ALU.mult, ALU.add).then_inc(s["emptied_dve"], 1)
                stack = Stack(None if l == 0 else 0)
                norm_scale(2 * l + 1)
                if l:
                    nc.vector.memset(col[:, 61:62], 0.0).then_inc(s["mixer_done"], 1)
                lower(stack, 0, 0)
                norm_empty(l, "fnorm", Q_GFFN)
                if l == 0:
                    dve.wait_ge(s["emptied_dve"], emptied(unit(l, "fnorm", 2))[1])
                    dve.wait_ge(s["xh_done"], 1)
                    tt(xl[:], hT[:], xh[:].bitcast(F32), ALU.subtract).then_inc(s["xl_done"], 1)
                if l == 0:
                    for j in range(1, AHEAD):
                        lower(stack, j, 0)
                    stream(stack, TT, False)
                    dve.wait_ge(s["piece_done"], 3 * NC_D)
                    for t in range(TT):
                        xs = X[:, t].rearrange("p (a n) -> p a n", a=2)
                        ins = tt(xs, xs, ps[:, 2 + 2 * t:4 + 2 * t], ALU.add)
                    ins.then_inc(s["dense_added"], 1)
                    dve.wait_ge(s["dense_added"], 1)

            dve.wait_ge(s["gain_in"], 16)
            full(unit(DEPTH - 1, "fnorm", 3))
            for t in range(TT):
                link(tt(hn[:, t], hn[:, t], ybuf[:], ALU.mult))
            dve.wait_ge(s["lg_done"], 1)
            e8 = cst[:, C_E8:C_E8 + 16].rearrange("p (a e) -> p a e", a=TT)
            lg, oh0, oh1, tmp, sel, gate = (rt[:, j] for j in range(6))

            def wide(c):
                return col[:, c:c + TT].rearrange("p (a b) -> p a b", b=1).to_broadcast([P, TT, NE])

            def largest(val, onehot):
                link(nc.vector.reduce_max(col[:, val:val + TT], lg, axis=AX.X))
                link(tt(tmp, lg, wide(val), ALU.is_equal))
                link(tt(tmp, tmp, e8, ALU.mult))
                link(nc.vector.tensor_reduce(col[:, 48:50], tmp, axis=AX.X, op=ALU.min))
                link(tt(onehot, e8, wide(48), ALU.is_equal))

            lgp = ps[:, 4, 0:TT * NE].rearrange("p (a e) -> p a e", a=TT)
            br = par[:, 0, Q_BR:Q_BR + NE].rearrange("p (a e) -> p a e", a=1).to_broadcast([P, TT, NE])
            link(tt(lg, lgp, br, ALU.add))
            largest(50, oh0)
            link(stt(lg, oh0, -3.0e38, lg, ALU.mult, ALU.add))
            largest(52, oh1)
            tt(col[:, 40:42], col[:, 52:54], col[:, 50:52], ALU.subtract).then_inc(s["routed_exp"], 1)
            tt(sel, oh0, oh1, ALU.add).then_inc(s["sel_ready"], 1)
            dve.wait_ge(s["ex_done"], 1)
            link(ts(col[:, 42:44], col[:, 44:46], 1.0, None, ALU.add))
            link(nc.vector.reciprocal(col[:, 54:56], col[:, 42:44]))
            link(tt(col[:, 56:58], col[:, 44:46], col[:, 54:56], ALU.mult))
            link(tt(gate, oh0, wide(54), ALU.mult))
            link(tt(tmp, oh1, wide(56), ALU.mult))
            link(tt(gate, gate, tmp, ALU.add))
            dve.wait_ge(s["pos_done"], 1)
            pos = ps[:, 5, 0:TT * NE].rearrange("p (a e) -> p a e", a=TT)
            link(ts(rt[:, 6], pos, 1.0, None, ALU.add))
            link(tt(rt[:, 6], rt[:, 6], sel, ALU.mult))
            link(ts(rt[:, 7], rt[:, 6], -1.0 - CAP, None, ALU.add))
            link(ts(rt[:, 6], rt[:, 6], -1.0, None, ALU.add))
            nc.vector.tensor_copy(cnt[:], ps[0:1, 5, TT * NE:TT * NE + NE]).then_inc(s["tables_ready"], 1)
            dve.wait_ge(s["tables_ready"], 1)

            def find(m, e, part, weighted):
                slot = cst[:, C_SLOT:C_SLOT + CAP]
                e = slice(e, e + 1) if isinstance(e, int) else bass.ds(e, 1)
                at_least(dve, "wt_done" if weighted else "gathered", m)
                for t in range(TT):
                    if weighted:
                        ins = ts(pick[:, 1, t], slot, rt[:, 6 + part, t, e], rt[:, 5, t, e], ALU.is_equal, ALU.mult)
                    else:
                        ins = ts(pick[:, 0, t], slot, rt[:, 6 + part, t, e], None, ALU.is_equal)
                ins.then_inc(s["weighed" if weighted else "picked"], 1)

            def gather(m):
                dve.wait_ge(s["xh_done"], m + 2)
                tt(xl[:, :, 0:CAP], ps[:, 4:6].rearrange("p b (a t) -> p (b a) t", a=4),
                   xh[:, :, 0:CAP].bitcast(F32), ALU.subtract).then_inc(s["xl_done"], 1)

            def add(m):
                for k in range(2 * TT):
                    dve.wait_ge(s["scattered"], 2 * TT * m + (k + 1))
                    xs = X[:, k // 2, (k % 2) * 512:(k % 2) * 512 + 512]
                    tt(xs, xs, ps[:, SCATTER[k]], ALU.add).then_inc(s["added"], 1)

            def expert(m, e, part, prev, more):
                def early():
                    if prev:
                        add(m - 1)
                    find(m, e, part, True)
                    if more:
                        find(m + 1, e + 1, 0, False)
                stack = Stack(m)
                stream(stack, 1, more, early, (lambda: gather(m + 1)) if more else None)
                dve.wait_ge(s["piece_done"], stack.piece(3 * NC_E, 0))
                nc.vector.tensor_copy(ybuf[:, 512:D], ps[:, 3]).then_inc(s["acc_dve"], 1)

            find(0, 0, 0, False)
            for j in range(1, AHEAD):
                lower(Stack(0), j, 0)
            gather(0)
            expert(0, 0, 0, False, True)
            with dve.Fori(1, NE - 1) as e:
                expert(e, e, 0, True, True)
            expert(NE - 1, NE - 1, 0, True, False)
            add(NE - 1)
            m = dve.alloc_register("dve_pass")
            dve.reg_mov(m, NE)
            with dve.Fori(0, NE) as e:
                c = dve.value_load(cnt[0:1, bass.ds(e, 1)], min_val=0, max_val=SEQ)
                with dve.If(c > CAP):
                    n = dve.snap(m, min_val=NE, max_val=2 * NE)
                    for j in range(AHEAD):
                        lower(Stack(n), j, 0)
                    find(n, e, 1, False)
                    gather(n)
                    expert(n, e, 1, False, False)
                    add(n)
                    dve.reg_add(m, m, 1)

            nc.vector.memset(col[:, 60:61], 0.0).then_inc(s["xh_ready"], 1)
            norm_scale(2 * DEPTH, "final_ready", ybuf)

        @block.tensor
        def _(pe):
            mm = nc.tensor.matmul

            def free(u):
                if u >= RINGN:
                    who, n = emptied(u - RINGN)
                    pe.wait_ge(s["emptied_act" if who == "A" else "emptied_dve"], n)

            def empty_wait(u):
                who, n = emptied(u)
                pe.wait_ge(s["emptied_act" if who == "A" else "emptied_dve"], n)

            def norm(l, stage, m):
                pe.wait_ge(s["hn_ready"], m + 1)
                for k in range(4):
                    u = unit(l, stage, k)
                    free(u)
                    for j in range(2):
                        for t in range(TT):
                            f = 2 * k + j
                            ins = nc.tensor.transpose(ps[:, bank(u), j * 256 + t * P:j * 256 + (t + 1) * P],
                                                      hn[:, t, f * P:(f + 1) * P], ident)
                    ins.then_inc(s["unit_done"], 1)

            def ht_ready(l, stage):
                empty_wait(unit(l, stage, 2))
                empty_wait(unit(l, stage, 3))

            def project(l, u, c, k):
                free(u)
                for j in range(2):
                    n = 2 * k + j
                    for f in range(KT):
                        ins = mm(ps[:, bank(u), j * 256:j * 256 + 256], mixw[:, c % 2, f, n * P:(n + 1) * P],
                                 hT[:, f, :], start=(f == 0), stop=(f == KT - 1))
                ins.then_inc(s["unit_done"], 1)
                return ins

            def bu(l, i):
                n = ST * l + i
                if n >= 2:
                    pe.wait_ge(s["bu_read"], n - 1)
                gp, d = i // 2, i % 2
                ft, q = gp // 4, 32 * (gp % 4)
                u = uT[q:q + 32, ft, ::-1] if d else uT[q:q + 32, ft, :]
                for r in range(2):
                    ins = mm(ps[:, i % 2, r * 256:r * 256 + 256], bw[q:q + 32, ft, d, r, :], u, start=True, stop=True,
                             tile_position=(q, 0))
                ins.then_inc(s["bu_ready"], 1)

            def outputs(l, i):
                n = ST * l + i
                gp, d = i // 2, i % 2
                ft, q = gp // 4, 32 * (gp % 4)
                if i % 8 == 0 and FT * l + ft >= 2:
                    pe.wait_ge(s["y_read"], FT * l + ft - 1)
                if added_here(i):
                    pe.wait_ge(s["summed"], N_ADDED * l + i + 1)
                else:
                    pe.wait_ge(s["products"], n + 1)
                addends = 1 if added_here(i) else 2
                for k in range(addends):
                    for r in range(2):
                        a = ro[:, i % 2, k, r, ::-1] if d else ro[:, i % 2, k, r, :]
                        ins = mm(ps[q:q + 32, 2 + ft % 2, 0:SEQ], cw[:, r, i, :], a,
                                 start=(d == 0 and k == 0 and r == 0),
                                 stop=(d == 1 and k == addends - 1 and r == 1), tile_position=(0, q))
                ins.then_inc(s["c_done"], 1)

            def attention(l, stage):
                u, h = unit(l, stage), int(stage.split(".")[0][-1])
                free(u)
                if stage[:3] == "map":
                    m = int(stage[-1])
                    if h == 0:
                        empty_wait(unit(l, "zqkv", 5))
                    r = slice(HD * m, HD * m + HD)
                    for q in range(TT):
                        ins = mm(ps[:, bank(u), q * 256:q * 256 + 256], qT[r, h, q * P:(q + 1) * P], kT[r, h, :],
                                 start=True, stop=True)
                elif stage[:4] == "turn":
                    pe.wait_ge(s["att_ready"], HEADS * l + h + 1)
                    for kt in range(TT):
                        for q in range(TT):
                            ins = nc.tensor.transpose(ps[:, bank(u), kt * 256 + q * P:kt * 256 + (q + 1) * P],
                                                      A[:, h % 2, q, kt * P:(kt + 1) * P], ident)
                elif stage[:4] == "head":
                    empty_wait(unit(l, f"turn{h}"))
                    for kt in range(TT):
                        ins = mm(ps[:, bank(u), 0:SEQ], v[:, kt, h * P:(h + 1) * P], AT[:, h % 2, kt],
                                 start=(kt == 0), stop=(kt == TT - 1))
                elif stage[:3] == "oms":
                    empty_wait(unit(l, f"head{2 * h + 1}"))
                    for a in range(2):
                        for t in range(TT):
                            c = TT * a + t
                            ins = mm(ps[:, bank(u), c:c + 1], osq[:, h, a, t * P:(t + 1) * P], ones[:, 0:1],
                                     start=True, stop=True)
                else:
                    k = int(stage[-1])
                    c, t = chunk(l, 4 + k % 2), k // 2
                    if h == 0 and k < 2:
                        mix_wait(pe, c)
                    ins = mm(ps[:, bank(u), :], cat[:, FT + h, t * P:(t + 1) * P], mixw[:, c % 2, FT + h, :],
                             start=True, stop=True)
                ins.then_inc(s["unit_done"], 1)

            def glu(l, k, fs):
                u = unit(l, "glu", k)
                if fs[0] == 0:
                    free(u)
                for f in fs:
                    for j in range(2):
                        n = 2 * k + j
                        ins = mm(ps[:, bank(u), j * 256:j * 256 + 256], wg[:, f, n * P:(n + 1) * P], yq[:, f],
                                 start=(f == 0 and j == 0), stop=(f == FT - 1 and j == 1))
                if fs[-1] == FT - 1:
                    ins.then_inc(s["unit_done"], 1)

            def output(l, k, fs):
                u = unit(l, "out", k)
                c, t = chunk(l, 4 + k % 2), k // 2
                if fs[0] == 0:
                    free(u)
                for f in fs:
                    ins = mm(ps[:, bank(u), :], cat[:, f, t * P:(t + 1) * P], mixw[:, c % 2, f, :],
                             start=(f == 0), stop=(f == FT - 1))
                if fs[-1] == FT - 1:
                    ins.then_inc(s["unit_done"], 1)

            def zqkv(l, k):
                u = unit(l, "zqkv", k)
                if k % 2 == 0:
                    mix_wait(pe, chunk(l, 1 + k // 2))
                if k < 4:
                    project(l, u, chunk(l, 1 + k // 2), k % 2)
                else:
                    free(u)
                    t = k - 4
                    for f in range(KT):
                        ins = mm(ps[:, bank(u), :], hT[:, f, t * P:(t + 1) * P], mixw[:, chunk(l, 3) % 2, f, :],
                                 start=(f == 0), stop=(f == KT - 1))
                    ins.then_inc(s["unit_done"], 1)

            def stream(stack, nt, after_b0=None, middle=None):
                halves = ((xh, wh), (xl, wh), (xh, wl))

                def turn(c, g):
                    pe.wait_ge(s["hv_ready"], stack.chunk(c, g) + 1)
                    for a in range(2):
                        for t in range(nt):
                            ins = nc.tensor.transpose(ps[:, 6, (a * nt + t) * P:(a * nt + t + 1) * P],
                                                      hv[:, t, a * P:(a + 1) * P], ident)
                    ins.then_inc(s["turned"], 1)

                def step(j, g, kind, c):
                    q, slot, k = stack.piece(j, g), stack.slot(j), stack.chunk(c, g)
                    if j == 3 * stack.n - 1:
                        turn(c, g)
                        if middle:
                            middle()
                    pe.wait_ge(s["lo_done"], q + 1)
                    if kind == "D":
                        pe.wait_ge(s["hid_lo"], k + 1)
                        first, last = j == 4 and isinstance(g, int) and g == 0, j == 3 * stack.n - 1
                        for a in range(2):
                            for t in range(nt):
                                for i, (x2, w2) in enumerate(((hidh, wh), (hidl, wh), (hidh, wl))):
                                    for n in range(2):
                                        at = a * D + n * 512
                                        ins = mm(ps[:, 2 + 2 * t + n], x2[:, a, t * P:(t + 1) * P],
                                                 w2[:, slot, at:at + 512], start=first and a == 0 and i == 0, stop=last and a == 1 and i == 2)
                        ins.then_inc(s["piece_done"], 1)
                        return
                    if kind == "A":
                        at_least(pe, "hv_ready", k if nt == TT else k - 1)
                    for t in range(nt):
                        b = t if nt == TT else c % 2
                        for f in range(4):
                            fx = f + (4 if kind == "B" else 0)
                            for i, (x2, w2) in enumerate(halves):
                                ins = mm(ps[:, b], x2[:, fx, t * P:(t + 1) * P], w2[:, slot, f * 512:(f + 1) * 512],
                                         start=(fx == 0 and i == 0), stop=(fx == KT - 1 and i == 2))
                    ins.then_inc(s["piece_done"], 1)
                    if kind == "A" and c:
                        turn(c - 1, g)
                    if j == 1 and after_b0:
                        after_b0()
                stack.walk(pe, step)

            for l in range(DEPTH):
                if l == 0:
                    pe.wait_ge(s["in_cst"], 16)
                norm(l, "norm", 2 * l)
                ht_ready(l, "norm")
                mix_wait(pe, chunk(l, 0))
                for k in range(2):
                    project(l, unit(l, "zu", k), chunk(l, 0), k)
                empty_wait(unit(l, "zu", 1))
                pe.wait_ge(s["in_b"], 16 * (l + 1))
                bu(l, 0)
                for i in range(ST):
                    if i + 1 < ST:
                        bu(l, i + 1)
                    if i in ZQKV_AT:
                        zqkv(l, ZQKV_AT.index(i))
                    for stage, _ in beside(i):
                        attention(l, stage)
                    if i == 1:
                        pe.wait_ge(s["cw_ready"], l + 1)
                    if i:
                        outputs(l, i - 1)
                pe.wait_ge(s["in_glu"], 16 * (l + 1))
                pe.wait_ge(s["g_ready"], FT * (l + 1) - 1)
                glu(l, 0, range(FT - 1))
                outputs(l, ST - 1)
                glu(l, 1, range(FT - 1))
                pe.wait_ge(s["g_ready"], FT * (l + 1))
                for k in range(2):
                    glu(l, k, range(FT - 1, FT))
                pe.wait_ge(s["cat_ready"], 2 * l + 1)
                for k in range(4):
                    output(l, k, range(FT // 2))
                pe.wait_ge(s["qs_ready"], l + 1)
                for t in range(TT):
                    for f in range(FT):
                        ins = mm(ps[:, 2, t:t + 1], th[:, f, t * P:(t + 1) * P], ones[:, 0:1], start=(f == 0),
                                 stop=(f == FT - 1))
                ins.then_inc(s["gss_done"], 1)
                for k in range(4):
                    output(l, k, range(FT // 2, FT))
                norm(l, "fnorm", 2 * l + 1)
                ht_ready(l, "fnorm")
                if l == 0:
                    pe.wait_ge(s["xl_done"], 1)
                    stream(Stack(None), TT)

            pe.wait_ge(s["in_wr"], 16)
            for t in range(TT):
                for f in range(KT):
                    ins = mm(ps[:, 4, t * NE:(t + 1) * NE], hT[:, f, t * P:(t + 1) * P], wr[:, f, :],
                             start=(f == 0), stop=(f == KT - 1))
            ins.then_inc(s["lg_done"], 1)
            pe.wait_ge(s["sel_ready"], 1)
            tri = cst[:, C_TRI:C_TRI + P]
            mm(ps[:, 5, 0:NE], tri, rt[:, 4, 0], start=True, stop=True)
            mm(ps[:, 5, NE:2 * NE], ones, rt[:, 4, 0], start=True, stop=False)
            mm(ps[:, 5, NE:2 * NE], tri, rt[:, 4, 1], start=False, stop=True)
            mm(ps[:, 5, 2 * NE:3 * NE], ones, rt[:, 4, 0], start=True, stop=False)
            mm(ps[:, 5, 2 * NE:3 * NE], ones, rt[:, 4, 1], start=False, stop=True).then_inc(s["pos_done"], 1)

            def gather(m, added):
                pe.wait_ge(s["picked"], m + 1)
                at_least(pe, "added", added)
                for f in range(KT):
                    for t in range(TT):
                        ins = mm(ps[:, 4 + f // 4, (f % 4) * P:(f % 4 + 1) * P], hn[:, t, f * P:(f + 1) * P],
                                 pick[:, 0, t], start=(t == 0), stop=(t == TT - 1))
                ins.then_inc(s["gathered"], 1)

            def scatter(m):
                pe.wait_ge(s["wt_ready"], m + 1)
                pe.wait_ge(s["acc_act"], m + 1)
                pe.wait_ge(s["acc_dve"], m + 1)
                for k in range(2 * TT):
                    if k == 3:
                        pe.wait_ge(s["added"], 2 * TT * m + 1)
                    t, n = k // 2, k % 2
                    mm(ps[:, SCATTER[k]], wT[:, t * P:(t + 1) * P], ybuf[:, n * 512:(n + 1) * 512],
                       start=True, stop=True).then_inc(s["scattered"], 1)

            def expert(m, prev, more):
                def middle():
                    pe.wait_ge(s["weighed"], m + 1)
                    if prev:
                        pe.wait_ge(s["added"], 2 * TT * m)
                    for t in range(TT):
                        ins = nc.tensor.transpose(ps[:, 7, t * P:(t + 1) * P], pick[:, 1, t], ident)
                    ins.then_inc(s["wt_done"], 1)
                    if more:
                        gather(m + 1, 2 * TT * m)
                pe.wait_ge(s["xl_done"], m + 2)
                stream(Stack(m), 1, (lambda: scatter(m - 1)) if prev else None, middle)

            gather(0, 0)
            expert(0, False, True)
            with pe.Fori(1, NE - 1) as e:
                expert(e, True, True)
            expert(NE - 1, True, False)
            scatter(NE - 1)
            pe.wait_ge(s["tables_ready"], 1)
            m = pe.alloc_register("pe_pass")
            pe.reg_mov(m, NE)
            with pe.Fori(0, NE) as e:
                c = pe.value_load(cnt[0:1, bass.ds(e, 1)], min_val=0, max_val=SEQ)
                with pe.If(c > CAP):
                    n = pe.snap(m, min_val=NE, max_val=2 * NE)
                    pe.wait_ge(s["added"], 2 * TT * n)
                    gather(n, 2 * TT * n)
                    expert(n, False, False)
                    scatter(n)
                    pe.reg_add(m, m, 1)


def constants():
    c = np.zeros((P, C_N), np.float32)
    p = np.arange(P)
    c[:, C_ID:C_ID + P] = np.eye(P)
    c[:, C_ONE:C_ONE + P] = 1.0
    c[:, C_TRI:C_TRI + P] = p[:, None] < p[None, :]
    for q in range(TT):
        c[:, C_DIST + q * SEQ:C_DIST + (q + 1) * SEQ] = np.abs(p[:, None] + q * P - np.arange(SEQ)[None, :])
    c[:, C_T:C_T + SEQ] = np.arange(SEQ)
    c[:, C_SLOT:C_SLOT + P] = p
    c[:, C_E8:C_E8 + 16] = np.tile(np.arange(NE) - NE, 2)
    return c


def kernel(**inputs):
    import concourse.bacc as bacc
    from concourse.bass_utils import run_bass_kernel_spmd

    a = {k: np.asarray(v) for k, v in inputs.items()}
    f32 = np.float32

    def by_feature(g, n):
        return g.reshape(DEPTH, n, P).transpose(0, 2, 1)

    def by_state(g):
        return g.reshape(DEPTH, 2, GP, 2, STATE).transpose(0, 3, 4, 2, 1).reshape(DEPTH, P, ST)

    def on_all(r):
        return np.broadcast_to(r[:, None, :], (r.shape[0], P, r.shape[1]))

    step = np.broadcast_to(a["ssm_log_step"][..., None], a["ssm_lambda_re"].shape)
    par = np.concatenate([
        by_feature(a["g_mix"], KT), by_feature(a["g_ffn"], KT), by_feature(a["ssm_d"], FT),
        by_feature(a["b_glu"], FT), by_feature(a["g_ssm_out"], FT), by_feature(a["g_subln"], 1),
        by_state(a["ssm_lambda_re"]), by_state(a["ssm_lambda_im"]), by_state(step),
        on_all(np.concatenate([a["lambda_q1"], a["lambda_k1"], a["lambda_q2"], a["lambda_k2"]], 1)),
        on_all(np.broadcast_to(a["b_router"], (DEPTH, NE)))], 2)
    rows = on_all(np.concatenate([a["g_ffn"][1], a["g_final"]])[None])[0]

    bmat = np.zeros((DEPTH, 4, 2, GROUP, FT, 2, 2, 2, STATE), f32)
    cmat = np.zeros((DEPTH, 2, STATE, 2, FT, 4, 2, 2, GROUP), f32)
    for r, (b, c) in enumerate((("ssm_b_re", "ssm_c_re"), ("ssm_b_im", "ssm_c_im"))):
        b6 = a[b].reshape(DEPTH, 2, FT, 4, 2, STATE, GROUP)
        c6 = a[c].reshape(DEPTH, 2, FT, 4, 2, GROUP, STATE)
        for g in range(2):
            bmat[:, :, g, :, :, :, r, g, :] = b6[:, :, :, :, g].transpose(0, 3, 5, 2, 1, 4)
            cmat[:, g, :, r, :, :, :, g, :] = c6[:, :, :, :, g].transpose(0, 5, 2, 3, 1, 4)
    bmat = bmat.reshape(DEPTH, P, FT, 2, 2, P)
    cmat = cmat.reshape(DEPTH, P, 2, ST, 32)

    def chunks(w, kt, n):
        return w.reshape(DEPTH, kt, P, n, 512).transpose(0, 3, 2, 1, 4)

    wmix = np.concatenate([chunks(a["w_in"], KT, 4), chunks(a["w_out"], KT, 2)], 1)
    wglu = chunks(a["w_glu"], FT, 1)[:, 0]
    wrouter = a["w_router"][0].reshape(KT, P, NE).transpose(1, 0, 2)

    def ffn(gate, up, down, nch):
        n, _, dff = gate.shape
        pad = ((0, 0), (0, 0), (0, nch * HC - dff))
        gu = np.stack([np.pad(w, pad).reshape(n, 2, 4, P, nch, HC) for w in (gate, up)])
        gu = gu.transpose(1, 5, 2, 4, 3, 0, 6).reshape(n, nch, 2, P, PIECE)
        dn = np.pad(down, ((0, 0), pad[2], (0, 0))).reshape(n, nch, 2, P, D).transpose(0, 1, 3, 2, 4)
        dn = dn.reshape(n, nch, P, PIECE)
        out = [gu[:, 0, 0], gu[:, 0, 1]]
        for c in range(1, nch):
            out += [gu[:, c, 0], gu[:, c, 1], dn[:, c - 1]]
        out.append(dn[:, nch - 1])
        return np.stack(out, 1).reshape(n * 3 * nch, P, PIECE)

    wffn = np.concatenate([
        ffn(a["dense_w_gate"], a["dense_w_up"], a["dense_w_down"], NC_D),
        ffn(a["moe_w_gate"][0], a["moe_w_up"][0], a["moe_w_down"][0], NC_E)])
    arrays = {
        "x_in": a["x"][0].reshape(TT, P, D).transpose(1, 0, 2),
        "consts": constants(), "rows": rows, "params": par.transpose(1, 0, 2), "bmat": bmat, "cmat": cmat,
        "wmix": wmix, "wglu": wglu, "wrouter": wrouter, "wffn": wffn,
    }
    arrays = {k: np.ascontiguousarray(v, dtype=f32) for k, v in arrays.items()}

    nc = bacc.Bacc("TRN2", target_bir_lowering=False, num_devices=1)
    aps = [nc.dram_tensor(k, v.shape, F32, kind="ExternalInput").ap() for k, v in arrays.items()]
    out = nc.dram_tensor("y_out", (P, TT, D), F32, kind="ExternalOutput").ap()
    encoder(nc, *aps, out)
    got = run_bass_kernel_spmd(nc, [arrays], core_ids=[0]).results[0]["y_out"]
    return np.ascontiguousarray(got.transpose(1, 0, 2)).reshape(1, SEQ, D)
```
